# Optimizing a Trainium2 kernel written in Bass

```python
import jax, jax.numpy as jnp
from jax import lax
import numpy as np

D_MODEL = 1024
BATCH = 1
SEQ = 256
DEPTH = 2

N_MIXERS = 2
WINDOWS = (128, 512, 2048)
DILATIONS = (1, 4, 16)
N_GROUPS = len(WINDOWS)
N_HEADS = 16
HEAD_DIM = D_MODEL // N_HEADS
ROPE_THETA = 10000.0
POOL_SIZES = (2, 4, 8, 16)
N_POOL_GROUPS = len(POOL_SIZES)
POOL_CH = D_MODEL // N_POOL_GROUPS
D_FF = ((8 * D_MODEL // 3 + 255) // 256) * 256
N_EXPERTS = 8
TOP_K = 2
D_FF_EXPERT = 7 * D_MODEL // 2
MOE_BLOCK = 256
RMS_EPS = 1e-6
MASK_VALUE = -1e30

kernel_name = 'hybrid_dilated_attn_pool_moe_trunk'

def rmsnorm(x, g):
    xf = x.astype(jnp.float32)
    y = xf * lax.rsqrt(jnp.mean(xf * xf, axis=-1, keepdims=True) + RMS_EPS)
    return (y * g.astype(jnp.float32)).astype(x.dtype)

def rope_tables(seq):
    pos = jnp.arange(seq, dtype=jnp.float32)
    inv_freq = ROPE_THETA ** (-jnp.arange(0, HEAD_DIM, 2, dtype=jnp.float32) / HEAD_DIM)
    ang = pos[:, None] * inv_freq[None, :]
    ang = jnp.concatenate([ang, ang], axis=-1)
    return jnp.cos(ang), jnp.sin(ang)

def apply_rope(t, cos, sin):
    half = HEAD_DIM // 2
    rot = jnp.concatenate([-t[..., half:], t[..., :half]], axis=-1)
    return t * cos[None, :, None, :] + rot * sin[None, :, None, :]

def dilated_window_attention(q, k, v, dilation, sub_window):
    B, S, H, Dh = q.shape
    d, W = dilation, sub_window
    L = S // d
    nb = -(-L // W)
    Lp = nb * W

    def to_sub(t):
        return t.reshape(B, L, d, H, Dh).transpose(0, 2, 3, 1, 4)

    qs = jnp.pad(to_sub(q), ((0, 0), (0, 0), (0, 0), (0, Lp - L), (0, 0)))
    qs = qs.reshape(B, d, H, nb, W, Dh)

    def key_blocks(t):
        tp = jnp.pad(to_sub(t), ((0, 0), (0, 0), (0, 0), (W, Lp - L), (0, 0)))
        tp = tp.reshape(B, d, H, nb + 1, W, Dh)
        return jnp.concatenate([tp[:, :, :, :-1], tp[:, :, :, 1:]], axis=4)

    kb = key_blocks(k)
    vb = key_blocks(v)
    scores = jnp.einsum('bdhnqe,bdhnke->bdhnqk', qs, kb)

    qi = jnp.arange(W)[None, :, None]
    kj = jnp.arange(2 * W)[None, None, :]
    blk = jnp.arange(nb)[:, None, None]
    dist = qi + W - kj
    valid = (dist >= 0) & (dist <= W) & (blk * W + kj - W >= 0)
    scores = jnp.where(valid, scores, MASK_VALUE)

    lse = jax.nn.logsumexp(scores, axis=-1)
    p = jnp.exp(scores - lse[..., None])
    o = jnp.einsum('bdhnqk,bdhnke->bdhnqe', p, vb)

    o = o.reshape(B, d, H, Lp, Dh)[:, :, :, :L]
    lse = lse.reshape(B, d, H, Lp)[:, :, :, :L]
    o = o.transpose(0, 3, 1, 2, 4).reshape(B, S, H, Dh)
    lse = lse.transpose(0, 3, 1, 2).reshape(B, S, H)
    return o, lse

def dilated_attention_mixer(h, w_qkv, w_o, cos, sin):
    B, S, D = h.shape
    qkv = (h @ w_qkv).astype(jnp.float32).reshape(B, S, N_GROUPS, 3, N_HEADS, HEAD_DIM)
    outs, lses = [], []
    for g in range(N_GROUPS):
        q = apply_rope(qkv[:, :, g, 0], cos, sin) * (HEAD_DIM ** -0.5)
        k = apply_rope(qkv[:, :, g, 1], cos, sin)
        v = qkv[:, :, g, 2]
        o, lse = dilated_window_attention(q, k, v, DILATIONS[g], WINDOWS[g] // DILATIONS[g])
        outs.append(o)
        lses.append(lse)
    wts = jax.nn.softmax(jnp.stack(lses, axis=0), axis=0)
    o = jnp.sum(wts[..., None] * jnp.stack(outs, axis=0), axis=0)
    return o.reshape(B, S, D).astype(h.dtype) @ w_o

def multiscale_pool_mixer(h, w_group, scale):
    B, S, D = h.shape
    hf = h.astype(jnp.float32)
    csum = jnp.concatenate([jnp.zeros((B, 1, D), jnp.float32), jnp.cumsum(hf, axis=1)], axis=1)
    t = jnp.arange(S)
    outs = []
    for g, P in enumerate(POOL_SIZES):
        sl = slice(g * POOL_CH, (g + 1) * POOL_CH)
        lo = jnp.maximum(t + 1 - P, 0)
        cnt = (t + 1 - lo).astype(jnp.float32)
        c_g = csum[:, :, sl]
        win_sum = c_g[:, 1:] - jnp.take(c_g, lo, axis=1)
        outs.append(win_sum / cnt[None, :, None] - hf[..., sl])
    y = jnp.stack(outs, axis=2)
    y = jnp.einsum('bsgc,gcd->bsgd', y, w_group.astype(jnp.float32)).reshape(B, S, D)
    return (y * scale.astype(jnp.float32)).astype(h.dtype)

def swiglu(h, w_gate, w_up, w_down):
    return (jax.nn.silu(h @ w_gate) * (h @ w_up)) @ w_down

def moe_swiglu(h, w_router, w_gate, w_up, w_down):
    B, S, D = h.shape
    N = B * S
    NK = N * TOP_K
    hf = h.reshape(N, D)
    logits = (hf @ w_router).astype(jnp.float32)
    top_val, top_idx = lax.top_k(logits, TOP_K)
    gates = jax.nn.softmax(top_val, axis=-1)

    flat_e = top_idx.reshape(NK).astype(jnp.int32)
    flat_t = jnp.repeat(jnp.arange(N, dtype=jnp.int32), TOP_K)
    flat_g = gates.reshape(NK)
    order = jnp.argsort(flat_e)
    e_s, t_s, g_s = flat_e[order], flat_t[order], flat_g[order]

    counts = jnp.bincount(flat_e, length=N_EXPERTS)
    starts = jnp.cumsum(counts) - counts
    padded = ((counts + MOE_BLOCK - 1) // MOE_BLOCK) * MOE_BLOCK
    pends = jnp.cumsum(padded)
    pstarts = pends - padded
    dest = pstarts[e_s] + (jnp.arange(NK, dtype=jnp.int32) - starts[e_s])

    n_blocks = -(-NK // MOE_BLOCK) + N_EXPERTS
    cap = n_blocks * MOE_BLOCK
    buf_tok = jnp.zeros((cap,), jnp.int32).at[dest].set(t_s)
    buf_gate = jnp.zeros((cap,), jnp.float32).at[dest].set(g_s)
    block_e = jnp.minimum(
        jnp.searchsorted(pends, jnp.arange(n_blocks) * MOE_BLOCK, side='right'),
        N_EXPERTS - 1).astype(jnp.int32)

    def run_block(args):
        tok, gate, e = args
        y = swiglu(hf[tok], w_gate[e], w_up[e], w_down[e])
        return y * gate[:, None].astype(y.dtype)

    y = lax.map(run_block, (buf_tok.reshape(n_blocks, MOE_BLOCK),
                            buf_gate.reshape(n_blocks, MOE_BLOCK), block_e))
    out = jnp.zeros((N, D), h.dtype).at[buf_tok].add(y.reshape(cap, D).astype(h.dtype))
    return out.reshape(B, S, D)

def setup_inputs(seed: int = 0) -> dict:
    key = jax.random.key(seed)
    ks = jax.random.split(key, 16)
    n_even = (DEPTH + 1) // 2
    n_odd = DEPTH // 2
    f32 = jnp.float32

    def nrm(k, shape, fan_in):
        return jax.random.normal(k, shape, f32) * (fan_in ** -0.5)

    def gain(k, shape):
        return 1.0 + 0.1 * jax.random.normal(k, shape, f32)

    return {
        'x': jax.random.normal(ks[0], (BATCH, SEQ, D_MODEL), f32),
        'mix_norm': gain(ks[1], (DEPTH, D_MODEL)),
        'ffn_norm': gain(ks[2], (DEPTH, D_MODEL)),
        'attn_w_qkv': nrm(ks[3], (n_even, D_MODEL, N_GROUPS * 3 * D_MODEL), D_MODEL),
        'attn_w_o': nrm(ks[4], (n_even, D_MODEL, D_MODEL), D_MODEL),
        'pool_w': nrm(ks[5], (n_odd, N_POOL_GROUPS, POOL_CH, POOL_CH), POOL_CH),
        'pool_scale': gain(ks[6], (n_odd, D_MODEL)),
        'dense_w_gate': nrm(ks[7], (n_even, D_MODEL, D_FF), D_MODEL),
        'dense_w_up': nrm(ks[8], (n_even, D_MODEL, D_FF), D_MODEL),
        'dense_w_down': nrm(ks[9], (n_even, D_FF, D_MODEL), D_FF),
        'moe_router': nrm(ks[10], (n_odd, D_MODEL, N_EXPERTS), D_MODEL),
        'moe_w_gate': nrm(ks[11], (n_odd, N_EXPERTS, D_MODEL, D_FF_EXPERT), D_MODEL),
        'moe_w_up': nrm(ks[12], (n_odd, N_EXPERTS, D_MODEL, D_FF_EXPERT), D_MODEL),
        'moe_w_down': nrm(ks[13], (n_odd, N_EXPERTS, D_FF_EXPERT, D_MODEL), D_FF_EXPERT),
        'final_norm': gain(ks[14], (D_MODEL,)),
    }

def reference(x, mix_norm, ffn_norm, attn_w_qkv, attn_w_o, pool_w, pool_scale,
              dense_w_gate, dense_w_up, dense_w_down, moe_router, moe_w_gate,
              moe_w_up, moe_w_down, final_norm):
    cos, sin = rope_tables(x.shape[1])
    for i in range(DEPTH):
        h = rmsnorm(x, mix_norm[i])
        j = i // N_MIXERS
        if i % N_MIXERS == 0:
            x = x + dilated_attention_mixer(h, attn_w_qkv[j], attn_w_o[j], cos, sin)
        else:
            x = x + multiscale_pool_mixer(h, pool_w[j], pool_scale[j])
        h = rmsnorm(x, ffn_norm[i])
        f = i // 2
        if i % 2 == 0:
            x = x + swiglu(h, dense_w_gate[f], dense_w_up[f], dense_w_down[f])
        else:
            x = x + moe_swiglu(h, moe_router[f], moe_w_gate[f], moe_w_up[f], moe_w_down[f])
    return rmsnorm(x, final_norm)


_drawn_inputs = setup_inputs


def setup_inputs(seed=0):
    import zlib

    import numpy as np

    out = dict(_drawn_inputs(seed))
    spreads = {}
    factors = {}
    for name, (base, spread) in spreads.items():
        noise = np.random.default_rng([zlib.crc32(name.encode()), seed]).standard_normal(out[name].shape)
        drawn = base * np.exp(spread * noise) if base else spread * noise
        out[name] = __import__('jax').numpy.asarray(drawn.astype(out[name].dtype))
    for name, factor in factors.items():
        out[name] = (out[name] * factor).astype(out[name].dtype)
    return out
```

```python
from contextlib import ExitStack

import concourse.bass as bass
from concourse import mybir

ALU = mybir.AluOpType
ACT = mybir.ActivationFunctionType
AX = mybir.AxisListType
F32 = mybir.dt.float32
F32R = mybir.dt.float32r
I32 = mybir.dt.int32

P = 128
SEQ = 256
TT = SEQ // P
D = 1024
KD = D // P
GROUPS = 3
HEADS = 16
HD = 64
QW = 256
QUARTERS = D // QW
QH = QW // HD
D_FF = 2816
FB = 256
N_FB = D_FF // FB
E = 8
D_FFE = 3584
EB = 512
N_EB = D_FFE // EB
POOL_SIZES = (2, 4, 8, 16)
PG = len(POOL_SIZES)
EPS = 1e-6
MASKED = -1e30
SCALE = HD ** -0.5

UNIT = 2048
RAW = 6
SPLIT = 3
N_QKV = QUARTERS * GROUPS * 3
U_WO = N_QKV
U_DENSE = U_WO + D // QW
U_POOL = U_DENSE + 3 * N_FB
U_MOE = U_POOL + 1
UE = 6 * N_EB
N_STEP = HEADS * TT

DENSE_SEQ = []
for _b in range(N_FB):
    DENSE_SEQ += [("gate", _b), ("up", _b)]
    if _b:
        DENSE_SEQ.append(("down", _b - 1))
DENSE_SEQ.append(("down", N_FB - 1))

MOE_SEQ = []
for _b in range(N_EB):
    MOE_SEQ += [("gate", _b, 0), ("gate", _b, 1), ("up", _b, 0), ("up", _b, 1)]
    if _b:
        MOE_SEQ += [("down", _b - 1, 0), ("down", _b - 1, 1)]
MOE_SEQ += [("down", N_EB - 1, 0), ("down", N_EB - 1, 1)]


def is_v(u):
    return u % 3 == 2


def qk_index(u):
    return 2 * (u // 3) + u % 3


def step_slot(n):
    return 3 * GROUPS * (n // (QH * TT) + 1) + n % (QH * TT)


STEP_AT = {step_slot(n): n for n in range(N_STEP)}
LAST_SLOT = step_slot(N_STEP - 1) + 3

START = 1

SCATTER = ((0, 0, 7), (0, 1, 6), (1, 0, 3), (1, 1, 5))


def program(nc, x_in, mix_norm, ffn_norm, w_qkv, w_o, pool_w, pool_scale, w_gate, w_up, w_down,
            router, e_gate, e_up, e_down, final_norm, mask_in, cos_in, sin_in, ident_in, iota_in,
            before_in, poolmat_in, out):
    ctx = ExitStack()
    with ctx:
        def sb(name, shape, dt=F32, scope=ctx):
            return scope.enter_context(nc.sbuf_tensor(name, shape, dt))

        def sem(name):
            return ctx.enter_context(nc.semaphore(name))

        raw = sb("raw", [P, RAW, UNIT])
        w_hi = sb("w_hi", [P, SPLIT, UNIT], F32R)
        w_lo = sb("w_lo", [P, SPLIT, UNIT], F32R)
        a_hi = sb("a_hi", [P, KD * SEQ], F32R)
        a_lo = sb("a_lo", [P, KD * SEQ], F32R)
        x = sb("x", [P, TT, D])
        hn = sb("hn", [P, TT, D])
        gains = sb("gains", [P, 3, D])
        ident = sb("ident", [P, P])
        iota = sb("iota", [P, SEQ])
        before = sb("before", [P, TT, SEQ])
        ones = sb("ones", [P, P])
        stat = sb("stat", [P, 16])
        route = sb("route", [P, TT, 8, E])
        posm = sb("posm", [P, TT, E])
        gate_w = sb("gate_w", [P, TT, E])
        rank3 = sb("rank3", [P, 2, E, E])
        tie = sb("tie", [P, E, E])
        over = sb("over", [P, E + 1])
        over_i = sb("over_i", [P, 1], I32)

        attn = ExitStack()
        qkT = sb("qkT", [P, 2, 2, GROUPS, 2, SEQ], F32, attn)
        v_sb = sb("v_sb", [P, 2, GROUPS, TT, QW], F32, attn)
        roped = sb("roped", [P, 2, TT, QW], F32, attn)
        rot = sb("rot", [P, 2, TT, QW], F32, attn)
        s_sb = sb("s_sb", [P, 2, 4 * P], F32, attn)
        e_sb = sb("e_sb", [P, 2, 4 * P], F32, attn)
        eT = sb("eT", [P, 2, 4 * P], F32, attn)
        mask = sb("mask", [P, TT, 4 * P], F32, attn)
        cos = sb("cos", [P, TT, HD], F32, attn)
        sin = sb("sin", [P, TT, HD], F32, attn)
        softs = sb("softs", [P, 2, 4], F32, attn)
        attn.close()

        dh = sb("dh", [P, TT, FB])
        dsg = sb("dsg", [P, TT, FB])
        dhT_hi = sb("dhT_hi", [P, 2, SEQ], F32R)
        dhT_lo = sb("dhT_lo", [P, 2, SEQ], F32R)
        poolmat = sb("poolmat", [P, PG, TT, SEQ])
        router_sb = sb("router_sb", [P, KD, E])
        hT = sb("hT", [P, KD, SEQ])
        xg_hi = sb("xg_hi", [P, KD, P], F32R)
        xg_lo = sb("xg_lo", [P, KD, P], F32R)
        sg = sb("sg", [P, EB])
        h = sb("h", [P, EB])
        hT_hi = sb("hT_hi", [P, 4, P], F32R)
        hT_lo = sb("hT_lo", [P, 4, P], F32R)
        pick = sb("pick", [P, TT, P], F32R)
        place = sb("place", [P, SEQ], F32R)
        y_hi = sb("y_hi", [P, D], F32R)
        y_lo = sb("y_lo", [P, D], F32R)

        ps = [ctx.enter_context(nc.psum_tensor(f"bank{n}", [P, 512], F32)) for n in range(8)]

        x_landed, gain0_landed, ident_landed = sem("x_landed"), sem("gain0_landed"), sem("ident_landed")
        consts_landed, late_landed = sem("consts_landed"), sem("late_landed")
        gain_scale, gain_ffn1, gain_final = sem("gain_scale"), sem("gain_ffn1"), sem("gain_final")
        raw_landed = [sem(f"raw_landed{n}") for n in range(RAW)]
        hi_ready, lo_ready, unit_used = sem("hi_ready"), sem("lo_ready"), sem("unit_used")
        ss_ready, var_ready, std_ready = sem("ss_ready"), sem("var_ready"), sem("std_ready")
        rstd_ready, hn_ready = sem("rstd_ready"), sem("hn_ready")
        tr_ready, a_hi_ready, a_lo_ready = sem("tr_ready"), sem("a_hi_ready"), sem("a_lo_ready")
        rope_read, rope_ready = sem("rope_read"), sem("rope_ready")
        v_ready, qkT_tr, qkT_ready = sem("v_ready"), sem("qkT_tr"), sem("qkT_ready")
        scores_ready, masked_ready = sem("scores_ready"), sem("masked_ready")
        bias_ready, exp_ready = sem("bias_ready"), sem("exp_ready")
        eT_tr, eT_ready, pv_ready = sem("eT_tr"), sem("eT_ready"), sem("pv_ready")
        rinv_ready, o_ready = sem("rinv_ready"), sem("o_ready")
        wo_added = sem("wo_added")
        dsilu_ready, dh_ready, dtr_ready = sem("dsilu_ready"), sem("dh_ready"), sem("dtr_ready")
        dhi_ready, dlo_ready, ffn_added = sem("dhi_ready"), sem("dlo_ready"), sem("ffn_added")
        pooled, pool_scaled, pool_added = sem("pooled"), sem("pool_scaled"), sem("pool_added")
        hnsplit_hi, hnsplit_lo = sem("hnsplit_hi"), sem("hnsplit_lo")
        hT_ready, logits_ready, route_step = sem("hT_ready"), sem("logits_ready"), sem("route_step")
        shifted_ready, weights_exp = sem("shifted_ready"), sem("weights_exp")
        sel_ready, prefix_ready, over_ready = sem("sel_ready"), sem("prefix_ready"), sem("over_ready")
        overs_summed, routed, tie_ready = sem("overs_summed"), sem("routed"), sem("tie_ready")
        pick_ready, gather_ready = sem("pick_ready"), sem("gather_ready")
        xg_hi_ready, xg_lo_ready = sem("xg_hi_ready"), sem("xg_lo_ready")
        silu_ready, h_ready, htr_ready = sem("silu_ready"), sem("h_ready"), sem("htr_ready")
        hT_hi_ready, hT_lo_ready = sem("hT_hi_ready"), sem("hT_lo_ready")
        place_tr, place_ready = sem("place_tr"), sem("place_ready")
        y_hi_ready, y_lo_ready = sem("y_hi_ready"), sem("y_lo_ready")
        scatter_ready, x_added, out_stored = sem("scatter_ready"), sem("x_added"), sem("out_stored")

        block = ctx.enter_context(nc.Block())

        def unit_source(u):
            if u < U_WO:
                c, g, part = u // 9, u % 9 // 3, u % 3
                n = (g * 3 + part) * D + c * QW
                return w_qkv[0, :, n:n + QW].rearrange("(k p) n -> p k n", p=P)
            if u < U_DENSE:
                n = (u - U_WO) * QW
                return w_o[0, :, n:n + QW].rearrange("(k p) n -> p k n", p=P)
            if u < U_POOL:
                kind, b = DENSE_SEQ[u - U_DENSE]
                if kind == "down":
                    return w_down[0, b * FB:(b + 1) * FB, :].rearrange("(k p) n -> p k n", p=P)
                w = w_gate if kind == "gate" else w_up
                return w[0, :, b * FB:(b + 1) * FB].rearrange("(k p) n -> p k n", p=P)
            return pool_w[0].rearrange("g (k p) n -> p (g k) n", p=P)

        def expert_source(j, e):
            kind, b, half = MOE_SEQ[j]
            if kind == "down":
                r = b * EB + half * 256
                return e_down[0, bass.ds(e, 1), r:r + 256, :].rearrange("a (k p) n -> p (a k) n", p=P)
            w = e_gate if kind == "gate" else e_up
            return w[0, bass.ds(e, 1), half * 512:(half + 1) * 512, b * EB:(b + 1) * EB]\
                .rearrange("a (k p) n -> p (a k) n", p=P)

        def raw_view(u, k):
            return raw[:, u % RAW, :].rearrange("p (k n) -> p k n", k=k)

        def split_hi(act, u, i=0):
            act.wait_ge(raw_landed[u % RAW], 16 * (u // RAW + 1) + 16 * (UE // RAW) * i)
            if u >= SPLIT:
                act.wait_ge(unit_used, u + 1 - SPLIT + UE * i)
            nc.scalar.activation(w_hi[:, u % SPLIT, :], raw[:, u % RAW, :], ACT.Copy).then_inc(hi_ready, 1)

        def split_lo(dve, u, i=0):
            dve.wait_ge(hi_ready, u + 1 + UE * i)
            nc.vector.tensor_tensor(w_lo[:, u % SPLIT, :], raw[:, u % RAW, :],
                                    w_hi[:, u % SPLIT, :].bitcast(F32), ALU.subtract).then_inc(lo_ready, 1)

        def halves(u, at, n):
            return w_hi[:, u % SPLIT, at:at + n], w_lo[:, u % SPLIT, at:at + n]

        def product(bank, hi, lo, w, start, stop):
            nc.tensor.matmul(bank, hi, w[0], start=start, stop=False)
            nc.tensor.matmul(bank, hi, w[1], start=False, stop=False)
            return nc.tensor.matmul(bank, lo, w[0], start=False, stop=stop)

        def act_of(k, t):
            c = slice(k * SEQ + t * P, k * SEQ + (t + 1) * P)
            return a_hi[:, c], a_lo[:, c]

        @block.sync
        def _(sp):
            sp.dma_start(x[:, :, :], x_in.rearrange("(t p) d -> p t d", p=P)).then_inc(x_landed, 16)
            for u in range(U_MOE):
                if u >= RAW:
                    sp.wait_ge(lo_ready, u - RAW + 1)
                src = unit_source(u)
                sp.dma_start(raw_view(u, src.shape[1]), src).then_inc(raw_landed[u % RAW], 16)

            def expert(i, e):
                for j in range(UE):
                    src = expert_source(j, e)
                    sp.wait_ge(lo_ready, U_MOE + j - RAW + 1 + i * UE)
                    sp.dma_start(raw_view(U_MOE + j, src.shape[1]), src)\
                        .then_inc(raw_landed[(U_MOE + j) % RAW], 16)

            with sp.Fori(0, E) as e:
                expert(e, e)
            sp.wait_ge(routed, 1)
            more = sp.value_load(over_i[0:1, 0:1], min_val=0, max_val=1)
            with sp.If(more != 0):
                with sp.Fori(0, E) as e:
                    expert(e + E, e)
            with sp.Else():
                sp.nop()
            for t in range(TT):
                sp.wait_ge(hn_ready, 4 * TT + t + 1)
                sp.dma_start(out[t * P:(t + 1) * P, :], hn[:, t, :]).then_inc(out_stored, 16)
            sp.wait_ge(out_stored, 16 * TT)

        @block.gpsimd
        def _(pool):
            nc.gpsimd.memset(ones[:, :], 1.0).then_inc(tie_ready, 1)
            for e in range(E):
                if e:
                    nc.gpsimd.memset(tie[:, e, 0:e], 1.0).then_inc(tie_ready, 1)
                nc.gpsimd.memset(tie[:, e, e:E], 0.0).then_inc(tie_ready, 1)
            for n in range(N_QKV * 2 // 3):
                pool.wait_ge(rope_read, n + 1)
                nc.gpsimd.tensor_tensor(roped[:, n % 2], roped[:, n % 2], rot[:, n % 2], ALU.add)\
                    .then_inc(rope_ready, 1)

            pool.wait_ge(hn_ready, TT)
            pool.dma_start(gains[:, 0, :], pool_scale[0:1, :].to_broadcast([P, D])).then_inc(gain_scale, 16)
            pool.wait_ge(o_ready, N_STEP)
            pool.dma_start(poolmat[:, :, :, :].rearrange("p g t n -> p (g t) n"),
                           poolmat_in.rearrange("g (t p) n -> p (g t) n", p=P)).then_inc(late_landed, 16)
            pool.dma_start(router_sb[:, :, :], router[0].rearrange("(k p) e -> p k e", p=P)).then_inc(late_landed, 16)
            pool.wait_ge(hn_ready, 2 * TT)
            pool.dma_start(gains[:, 1, :], ffn_norm[1:2, :].to_broadcast([P, D])).then_inc(gain_ffn1, 16)
            pool.wait_ge(hn_ready, 3 * TT)
            pool.dma_start(gains[:, 2, :], final_norm.rearrange("(a n) -> a n", a=1).to_broadcast([P, D]))\
                .then_inc(gain_final, 16)

        MEMSETS = 2 * E

        @block.scalar
        def _(act):
            for n, (dst, src) in enumerate([(ident[:, :], ident_in), (gains[:, 0, :], mix_norm[0:1, :].to_broadcast([P, D]))]):
                act.dma_start(dst, src).then_inc((ident_landed, gain0_landed)[n], 16)
            for dst, src in ((cos[:, :, :], cos_in.rearrange("(t p) d -> p t d", p=P)),
                             (sin[:, :, :], sin_in.rearrange("(t p) d -> p t d", p=P)),
                             (mask[:, :, :], mask_in.rearrange("t p d -> p t d")),
                             (iota[:, :], iota_in),
                             (before[:, :, :], before_in.rearrange("(t p) d -> p t d", p=P)),
                             (gains[:, 1, :], ffn_norm[0:1, :].to_broadcast([P, D])),
                             (gains[:, 2, :], mix_norm[1:2, :].to_broadcast([P, D]))):
                act.dma_start(dst, src).then_inc(consts_landed, 16)

            def norm(m):
                for t in range(TT):
                    nc.scalar.activation(hn[:, t, :], x[:, t, :], ACT.Square, accum_out=stat[:, t:t + 1])\
                        .then_inc(ss_ready, 1)
                act.wait_ge(var_ready, m + 1)
                nc.scalar.activation(stat[:, 4:4 + TT], stat[:, 2:2 + TT], ACT.Sqrt).then_inc(std_ready, 1)

            def split_banks(m):
                for j in range(4):
                    act.wait_ge(tr_ready, 4 * m + j + 1)
                    nc.scalar.activation(a_hi[:, j * 512:(j + 1) * 512], ps[4 + j][:, :], ACT.Copy)\
                        .then_inc(a_hi_ready, 1)

            act.wait_ge(x_landed, 16)
            norm(0)
            split_banks(0)
            split_hi(act, 0)
            split_hi(act, 1)

            for s in range(LAST_SLOT + 1):
                u = s - 1
                if 0 <= u < N_QKV and is_v(u):
                    g, c = u % 9 // 3, u // 9
                    act.wait_ge(unit_used, u + 1)
                    if c >= 2:
                        act.wait_ge(pv_ready, QH * TT * (c - 1))
                    nc.scalar.activation(v_sb[:, c % 2, g], ps[u % 2][:, :].rearrange("p (t n) -> p t n", t=TT),
                                         ACT.Copy).then_inc(v_ready, 1)
                u = s - 2
                if 0 <= u < N_QKV and not is_v(u):
                    g, c = u % 9 // 3, u // 9
                    act.wait_ge(qkT_tr, qk_index(u) + 1)
                    if c >= 2:
                        act.wait_ge(scores_ready, QH * TT * (c - 1))
                    nc.scalar.activation(qkT[:, c % 2, u % 3, g].rearrange("p a t -> p (a t)"), ps[2][:, :],
                                         ACT.Copy).then_inc(qkT_ready, 1)
                n = STEP_AT.get(s - 2)
                if n is not None:
                    act.wait_ge(eT_tr, n + 1)
                    if n >= 2:
                        act.wait_ge(pv_ready, n - 1)
                    nc.scalar.activation(eT[:, n % 2, :], ps[5 + n % 2][:, :], ACT.Copy).then_inc(eT_ready, 1)
                n = STEP_AT.get(s - 1)
                if n is not None:
                    act.wait_ge(bias_ready, n + 1)
                    if n >= 2:
                        act.wait_ge(eT_tr, n - 1)
                        act.wait_ge(rinv_ready, n - 1)
                    nc.scalar.activation(e_sb[:, n % 2, :], s_sb[:, n % 2, :], ACT.Exp, scale=SCALE,
                                         bias=softs[:, n % 2, 1:2], accum_out=softs[:, n % 2, 2:3])\
                        .then_inc(exp_ready, 1)
                if s < N_QKV + 1:
                    split_hi(act, s + 2)

            split_banks(1)
            for u in range(U_WO + 1, U_DENSE):
                split_hi(act, u + 2)

            act.wait_ge(wo_added, QUARTERS)
            norm(1)
            split_banks(2)

            for s, (kind, b) in enumerate(DENSE_SEQ):
                if kind == "up":
                    act.wait_ge(unit_used, U_DENSE + s)
                    if b:
                        act.wait_ge(dh_ready, b)
                    nc.scalar.activation(dsg[:, :, :], ps[4][:, :].rearrange("p (t n) -> p t n", t=TT), ACT.Silu)\
                        .then_inc(dsilu_ready, 1)
                if (kind == "gate" and b) or s == len(DENSE_SEQ) - 1:
                    d = b - 1 if kind == "gate" else b
                    act.wait_ge(dtr_ready, d + 1)
                    nc.scalar.activation(dhT_hi[:, :, :], ps[6][:, :].rearrange("p (k t) -> p k t", k=2), ACT.Copy)\
                        .then_inc(dhi_ready, 1)
                if U_DENSE + s + 2 < U_MOE:
                    split_hi(act, U_DENSE + s + 2)
            split_hi(act, U_MOE)

            act.wait_ge(ffn_added, 4)
            norm(2)
            split_banks(3)
            split_hi(act, U_MOE + 1)

            act.wait_ge(pool_added, 4)
            norm(3)
            for t in range(TT):
                act.wait_ge(hn_ready, 3 * TT + t + 1)
                nc.scalar.activation(a_hi[:, t * D:(t + 1) * D], hn[:, t, :], ACT.Copy).then_inc(hnsplit_hi, 1)
            for j in range(4):
                act.wait_ge(tr_ready, 4 * 4 + j + 1)
                nc.scalar.activation(hT[:, 2 * j:2 * j + 2, :], ps[4 + j][:, :].rearrange("p (k t) -> p k t", k=2),
                                     ACT.Copy).then_inc(hT_ready, 1)
            act.wait_ge(shifted_ready, 1)
            nc.scalar.activation(route[:, :, 2, :], route[:, :, 1, :], ACT.Exp).then_inc(weights_exp, 1)

            def gather(g):
                for n in range(2):
                    act.wait_ge(gather_ready, 4 * g + n + 1)
                    nc.scalar.activation(xg_hi[:, 4 * n:4 * n + 4, :],
                                         ps[(3, 5)[n]][:, :].rearrange("p (k s) -> p k s", k=4), ACT.Copy)\
                        .then_inc(xg_hi_ready, 1)

            def expert(i, last):
                at = U_MOE + i * UE
                for j, (kind, b, half) in enumerate(MOE_SEQ):
                    blk = i * N_EB + b
                    if kind == "up" and half == 0:
                        act.wait_ge(unit_used, at + j)
                        act.wait_ge(h_ready, START + blk)
                        nc.scalar.activation(sg[:, :], ps[2 + b % 2][:, :], ACT.Silu).then_inc(silu_ready, 1)
                    if (kind == "gate" and half == 1 and b) or (kind == "down" and b == N_EB - 1 and half == 0):
                        d = blk - 1 if kind == "gate" else blk
                        act.wait_ge(htr_ready, START + d + 1)
                        nc.scalar.activation(hT_hi[:, :, :], ps[6][:, :].rearrange("p (k s) -> p k s", k=4), ACT.Copy)\
                            .then_inc(hT_hi_ready, 1)
                        if kind == "down" and not last:
                            gather(i + 1)
                    if (kind, b, half) == ("up", 1, 1):
                        act.wait_ge(place_tr, i + 1)
                        nc.scalar.activation(place[:, :], ps[7][:, 0:SEQ], ACT.Copy).then_inc(place_ready, 1)
                    if j + 2 < UE or not last:
                        split_hi(act, U_MOE + j + 2, i)
                act.wait_ge(unit_used, at + UE)
                for n in range(2):
                    nc.scalar.activation(y_hi[:, n * 512:(n + 1) * 512], ps[n][:, :], ACT.Copy)\
                        .then_inc(y_hi_ready, 1)

            def round_of_experts(first):
                gather(first)
                with act.Fori(0, E - 1) as e:
                    expert(e + first, False)
                expert(first + E - 1, True)
                act.wait_ge(x_added, START + 4 * (first + E))

            round_of_experts(0)
            act.wait_ge(routed, 1)
            more = act.value_load(over_i[0:1, 0:1], min_val=0, max_val=1)
            with act.If(more != 0):
                split_hi(act, U_MOE + E * UE)
                split_hi(act, U_MOE + E * UE + 1)
                round_of_experts(E)
                act.nop()
            with act.Else():
                act.nop()
            norm(4)

        @block.vector
        def _(dve):
            dve.wait_ge(tie_ready, MEMSETS)

            def norm(m, gain, landed, count):
                dve.wait_ge(ss_ready, TT * (m + 1))
                nc.vector.tensor_scalar(stat[:, 2:2 + TT], stat[:, 0:TT], 1.0 / D, EPS, ALU.mult, ALU.add)\
                    .then_inc(var_ready, 1)
                dve.wait_ge(std_ready, m + 1)
                nc.vector.reciprocal(stat[:, 6:6 + TT], stat[:, 4:4 + TT]).then_inc(rstd_ready, 1)
                dve.wait_ge(rstd_ready, m + 1)
                dve.wait_ge(landed, count)
                for t in range(TT):
                    nc.vector.scalar_tensor_tensor(hn[:, t, :], x[:, t, :], stat[:, 6 + t:7 + t], gains[:, gain, :],
                                                   ALU.mult, ALU.mult).then_inc(hn_ready, 1)

            def split_banks(m):
                for j in range(4):
                    dve.wait_ge(a_hi_ready, 4 * m + j + 1)
                    nc.vector.tensor_tensor(a_lo[:, j * 512:(j + 1) * 512], ps[4 + j][:, :],
                                            a_hi[:, j * 512:(j + 1) * 512].bitcast(F32), ALU.subtract)\
                        .then_inc(a_lo_ready, 1)

            dve.wait_ge(x_landed, 16)
            norm(0, 0, gain0_landed, 16)
            split_banks(0)
            split_lo(dve, 0)
            split_lo(dve, 1)
            dve.wait_ge(consts_landed, 16 * 7)

            for s in range(LAST_SLOT + 1):
                n = STEP_AT.get(s - 3)
                if n is not None:
                    t, head = n % TT, n // TT
                    dve.wait_ge(pv_ready, n + 1)
                    nc.vector.reciprocal(softs[:, n % 2, 3:4], softs[:, n % 2, 2:3]).then_inc(rinv_ready, 1)
                    dve.wait_ge(rinv_ready, n + 1)
                    nc.vector.tensor_scalar(hn[:, t, head * HD:(head + 1) * HD], ps[7][:, 0:HD],
                                            softs[:, n % 2, 3:4], None, ALU.mult).then_inc(o_ready, 1)
                u = s - 1
                if 0 <= u < N_QKV and not is_v(u):
                    q = qk_index(u)
                    dve.wait_ge(unit_used, u + 1)
                    if q >= 2:
                        dve.wait_ge(qkT_tr, q - 1)
                        dve.wait_ge(rope_ready, q - 1)
                    bank = ps[u % 2][:, :].rearrange("p (t a n) -> p t a n", t=TT, a=QH)
                    dst = roped[:, q % 2].rearrange("p t (a n) -> p t a n", a=QH)
                    turned = rot[:, q % 2].rearrange("p t (a n) -> p t a n", a=QH)
                    h2 = HD // 2
                    for t in range(TT):
                        nc.vector.tensor_tensor(dst[:, t], bank[:, t],
                                                cos[:, t, :].unsqueeze(1).to_broadcast([P, QH, HD]), ALU.mult)
                        for lo, hi in ((0, h2), (h2, 0)):
                            last = nc.vector.tensor_tensor(
                                turned[:, t, :, lo:lo + h2], bank[:, t, :, hi:hi + h2],
                                sin[:, t, lo:lo + h2].unsqueeze(1).to_broadcast([P, QH, h2]), ALU.mult)
                    last.then_inc(rope_read, 1)
                n = STEP_AT.get(s - 1)
                if n is not None:
                    dve.wait_ge(scores_ready, n + 1)
                    if n >= 2:
                        dve.wait_ge(exp_ready, n - 1)
                        dve.wait_ge(o_ready, n - 1)
                    nc.vector.tensor_tensor_reduce(out=s_sb[:, n % 2, :], in0=ps[3 + n % 2][:, :], in1=mask[:, n % TT, :],
                                                   scale=1.0, scalar=-3e38, op0=ALU.add, op1=ALU.max,
                                                   accum_out=softs[:, n % 2, 0:1]).then_inc(masked_ready, 1)
                    dve.wait_ge(masked_ready, n + 1)
                    nc.vector.tensor_scalar(softs[:, n % 2, 1:2], softs[:, n % 2, 0:1], -SCALE, None, ALU.mult)\
                        .then_inc(bias_ready, 1)
                if s < N_QKV + 1:
                    split_lo(dve, s + 2)

            split_banks(1)
            for n in range(QUARTERS):
                dve.wait_ge(unit_used, U_WO + n + 1)
                cols = x[:, :, n * QW:(n + 1) * QW]
                nc.vector.tensor_tensor(cols, cols, ps[n % 2][:, :].rearrange("p (t n) -> p t n", t=TT), ALU.add)\
                    .then_inc(wo_added, 1)
                if n < QUARTERS - 1:
                    split_lo(dve, U_WO + n + 3)
            norm(1, 1, consts_landed, 16 * 7)
            split_banks(2)

            for s, (kind, b) in enumerate(DENSE_SEQ):
                if s and DENSE_SEQ[s - 1][0] == "up":
                    d = DENSE_SEQ[s - 1][1]
                    dve.wait_ge(unit_used, U_DENSE + s)
                    dve.wait_ge(dsilu_ready, d + 1)
                    if d:
                        dve.wait_ge(dtr_ready, d)
                    nc.vector.tensor_tensor(dh[:, :, :], dsg[:, :, :], ps[5][:, :].rearrange("p (t n) -> p t n", t=TT),
                                            ALU.mult).then_inc(dh_ready, 1)
                if (kind == "gate" and b) or s == len(DENSE_SEQ) - 1:
                    d = b - 1 if kind == "gate" else b
                    dve.wait_ge(dhi_ready, d + 1)
                    nc.vector.tensor_tensor(dhT_lo[:, :, :], ps[6][:, :].rearrange("p (k t) -> p k t", k=2),
                                            dhT_hi[:, :, :].bitcast(F32), ALU.subtract).then_inc(dlo_ready, 1)
                if U_DENSE + s + 2 < U_MOE:
                    split_lo(dve, U_DENSE + s + 2)
            split_lo(dve, U_MOE)
            dve.wait_ge(unit_used, U_POOL)
            for t in range(TT):
                for n in range(2):
                    cols = x[:, t, n * 512:(n + 1) * 512]
                    nc.vector.tensor_tensor(cols, cols, ps[2 * t + n][:, :], ALU.add).then_inc(ffn_added, 1)
            norm(2, 2, consts_landed, 16 * 7)
            split_banks(3)
            split_lo(dve, U_MOE + 1)

            dve.wait_ge(unit_used, U_POOL + 1)
            dve.wait_ge(gain_scale, 16)
            for t in range(TT):
                for n in range(2):
                    q = 2 * t + n
                    cols = slice(n * 512, (n + 1) * 512)
                    nc.vector.tensor_tensor(hn[:, t, cols], ps[q][:, :], gains[:, 0, cols], ALU.mult)\
                        .then_inc(pool_scaled, 1)
                    dve.wait_ge(pool_scaled, q + 1)
                    nc.vector.tensor_tensor(x[:, t, cols], x[:, t, cols], hn[:, t, cols], ALU.add)\
                        .then_inc(pool_added, 1)
            norm(3, 1, gain_ffn1, 16)
            for t in range(TT):
                dve.wait_ge(hnsplit_hi, t + 1)
                nc.vector.tensor_tensor(a_lo[:, t * D:(t + 1) * D], hn[:, t, :], a_hi[:, t * D:(t + 1) * D].bitcast(F32),
                                        ALU.subtract).then_inc(hnsplit_lo, 1)

            steps = [0]

            def chain(instruction):
                steps[0] += 1
                instruction.then_inc(route_step, 1)
                dve.wait_ge(route_step, steps[0])

            dve.wait_ge(logits_ready, 1)
            lg, shifted, ex, rank, sel, wt, pos, far = (route[:, :, n, :] for n in range(8))
            chain(nc.vector.tensor_copy(lg, ps[0][:, 0:TT * E].rearrange("p (t e) -> p t e", t=TT)))
            chain(nc.vector.tensor_reduce(stat[:, 8:8 + TT], lg, AX.X, ALU.max))
            nc.vector.tensor_tensor(shifted, lg, stat[:, 8:8 + TT].unsqueeze(2).to_broadcast([P, TT, E]), ALU.subtract)\
                .then_inc(shifted_ready, 1)
            for t in range(TT):
                other = lg[:, t, :].unsqueeze(1).to_broadcast([P, E, E])
                own = lg[:, t, :].unsqueeze(2).to_broadcast([P, E, E])
                chain(nc.vector.tensor_tensor(rank3[:, 1], other, own, ALU.is_equal))
                chain(nc.vector.tensor_tensor(rank3[:, 1], rank3[:, 1], tie[:, :, :], ALU.mult))
                chain(nc.vector.tensor_tensor(rank3[:, 0], other, own, ALU.is_gt))
                chain(nc.vector.tensor_tensor(rank3[:, 0], rank3[:, 0], rank3[:, 1], ALU.add))
                chain(nc.vector.tensor_reduce(rank[:, t, :], rank3[:, 0], AX.X, ALU.add))
            nc.vector.tensor_scalar(sel, rank, 2.0, None, ALU.is_lt).then_inc(sel_ready, 1)
            dve.wait_ge(sel_ready, 1)
            dve.wait_ge(weights_exp, 1)
            chain(nc.vector.tensor_tensor(wt, ex, sel, ALU.mult))
            chain(nc.vector.tensor_reduce(stat[:, 10:10 + TT], wt, AX.X, ALU.add))
            chain(nc.vector.reciprocal(stat[:, 12:12 + TT], stat[:, 10:10 + TT]))
            chain(nc.vector.tensor_tensor(gate_w[:, :, :], wt, stat[:, 12:12 + TT].unsqueeze(2).to_broadcast([P, TT, E]),
                                          ALU.mult))
            dve.wait_ge(prefix_ready, 1)
            chain(nc.vector.scalar_tensor_tensor(pos, ps[1][:, 0:TT * E].rearrange("p (t e) -> p t e", t=TT), 1.0,
                                                 sel, ALU.add, ALU.mult))
            chain(nc.vector.tensor_scalar(posm[:, :, :], pos, -1.0, None, ALU.add))
            chain(nc.vector.tensor_scalar(far, posm[:, :, :], float(P), None, ALU.is_ge))
            nc.vector.tensor_reduce(over[:, 0:1], far, AX.XY, ALU.add).then_inc(over_ready, 1)
            dve.wait_ge(overs_summed, 1)
            nc.vector.tensor_scalar(over_i[:, :], ps[2][:, 0:1], 1.0, None, ALU.min).then_inc(routed, 1)

            def pick_slots(i, first):
                shift = 0 if first == 0 else P
                for t in range(TT):
                    nc.vector.tensor_scalar(pick[:, t, :], iota[:, shift:shift + P], posm[:, t, bass.ds(i - first, 1)],
                                            None, ALU.is_equal).then_inc(pick_ready, 1)

            def gather(g):
                for n in range(2):
                    dve.wait_ge(gather_ready, 4 * g + 3 + n)
                    nc.vector.tensor_copy(xg_lo[:, 4 * n:4 * n + 4, :],
                                          ps[(2, 4)[n]][:, :].rearrange("p (k s) -> p k s", k=4)).then_inc(xg_lo_ready, 1)

            def expert(i, first, last):
                at = U_MOE + i * UE
                for j, (kind, b, half) in enumerate(MOE_SEQ):
                    if j and MOE_SEQ[j - 1][0] == "up" and MOE_SEQ[j - 1][2] == 1:
                        d = MOE_SEQ[j - 1][1] + i * N_EB
                        dve.wait_ge(unit_used, at + j)
                        dve.wait_ge(silu_ready, d + 1)
                        dve.wait_ge(htr_ready, START + d)
                        nc.vector.tensor_tensor(h[:, :], sg[:, :], ps[4 + MOE_SEQ[j - 1][1] % 2][:, :], ALU.mult)\
                            .then_inc(h_ready, 1)
                    if (kind == "gate" and half == 1 and b) or (kind == "down" and b == N_EB - 1 and half == 0):
                        d = i * N_EB + (b - 1 if kind == "gate" else b)
                        dve.wait_ge(hT_hi_ready, d + 1)
                        nc.vector.tensor_tensor(hT_lo[:, :, :], ps[6][:, :].rearrange("p (k s) -> p k s", k=4),
                                                hT_hi[:, :, :].bitcast(F32), ALU.subtract).then_inc(hT_lo_ready, 1)
                        if kind == "down" and not last:
                            gather(i + 1)
                    if (kind, b, half) == ("gate", 3, 0) and not last:
                        dve.wait_ge(place_tr, i + 1)
                        pick_slots(i + 1, first)
                    if j + 2 < UE or not last:
                        split_lo(dve, U_MOE + j + 2, i)
                for n in range(2):
                    dve.wait_ge(y_hi_ready, 2 * i + n + 1)
                    cols = slice(n * 512, (n + 1) * 512)
                    nc.vector.tensor_tensor(y_lo[:, cols], ps[n][:, :], y_hi[:, cols].bitcast(F32), ALU.subtract)\
                        .then_inc(y_lo_ready, 1)
                for q, (n, t, bank) in enumerate(SCATTER):
                    dve.wait_ge(scatter_ready, 4 * i + q + 1)
                    cols = x[:, t, n * 512:(n + 1) * 512]
                    nc.vector.scalar_tensor_tensor(cols, ps[bank][:, :], gate_w[:, t, bass.ds(i - first, 1)], cols,
                                                   ALU.mult, ALU.add).then_inc(x_added, 1)

            def round_of_experts(first):
                pick_slots(first, first)
                gather(first)
                with dve.Fori(0, E - 1) as e:
                    expert(e + first, first, False)
                expert(first + E - 1, first, True)
                dve.wait_ge(x_added, START + 4 * (first + E))

            for counter in (h_ready, hT_lo_ready, x_added, y_lo_ready):
                dve.sem_inc(counter, START)
            round_of_experts(0)
            more = dve.value_load(over_i[0:1, 0:1], min_val=0, max_val=1)
            with dve.If(more != 0):
                split_lo(dve, U_MOE + E * UE)
                split_lo(dve, U_MOE + E * UE + 1)
                round_of_experts(E)
                dve.nop()
            with dve.Else():
                dve.nop()
            norm(4, 2, gain_final, 16)

        @block.tensor
        def _(pe):
            def turn(m, src):
                for j in range(4):
                    for k in range(2):
                        for t in range(TT):
                            c = (2 * j + k) * P
                            last = nc.tensor.transpose(ps[4 + j][:, k * SEQ + t * P:k * SEQ + (t + 1) * P],
                                                       src[:, t, c:c + P], ident[:, :])
                    last.then_inc(tr_ready, 1)

            def full_unit(u, bank):
                for t in range(TT):
                    for k in range(KD):
                        hi, lo = act_of(k, t)
                        last = product(bank[:, t * QW:(t + 1) * QW], hi, lo, halves(u, k * QW, QW), k == 0, k == KD - 1)
                last.then_inc(unit_used, 1)

            pe.wait_ge(ident_landed, 16)
            pe.wait_ge(hn_ready, TT)
            turn(0, hn)
            pe.wait_ge(a_lo_ready, 4)

            for s in range(LAST_SLOT + 1):
                if s < N_QKV:
                    pe.wait_ge(lo_ready, s + 1)
                    if s >= 2 and is_v(s - 2):
                        pe.wait_ge(v_ready, (s - 2) // 3 + 1)
                    elif s >= 2:
                        pe.wait_ge(rope_read, qk_index(s - 2) + 1)
                    full_unit(s, ps[s % 2])
                u = s - 1
                if 0 <= u < N_QKV and not is_v(u):
                    q = qk_index(u)
                    pe.wait_ge(rope_ready, q + 1)
                    if q:
                        pe.wait_ge(qkT_ready, q)
                    for pair in range(2):
                        for t in range(TT):
                            c = pair * SEQ + t * P
                            last = nc.tensor.transpose(ps[2][:, c:c + P], roped[:, q % 2, t, pair * P:(pair + 1) * P],
                                                       ident[:, :])
                    last.then_inc(qkT_tr, 1)
                n = STEP_AT.get(s - 2)
                if n is not None:
                    t, c, hh = n % TT, n // (QH * TT), n // TT % QH
                    pe.wait_ge(eT_ready, n + 1)
                    if n:
                        pe.wait_ge(o_ready, n)
                    for k, (g, kt) in enumerate(((0, 0), (0, 1), (1, t), (2, t))):
                        last = nc.tensor.matmul(ps[7][:, 0:HD], eT[:, n % 2, k * P:(k + 1) * P],
                                                v_sb[:, c % 2, g, kt, hh * HD:(hh + 1) * HD], start=k == 0, stop=k == 3)
                    last.then_inc(pv_ready, 1)
                n = STEP_AT.get(s - 1)
                if n is not None:
                    pe.wait_ge(exp_ready, n + 1)
                    if n >= 2:
                        pe.wait_ge(eT_ready, n - 1)
                    for k in range(4):
                        last = nc.tensor.transpose(ps[5 + n % 2][:, k * P:(k + 1) * P], e_sb[:, n % 2, k * P:(k + 1) * P],
                                                   ident[:, :])
                    last.then_inc(eT_tr, 1)
                n = STEP_AT.get(s)
                if n is not None:
                    t, c, hh = n % TT, n // (QH * TT), n // TT % QH
                    if n % (QH * TT) == 0:
                        pe.wait_ge(qkT_ready, 2 * GROUPS * (c + 1))
                        pe.wait_ge(v_ready, GROUPS * (c + 1))
                    if n >= 2:
                        pe.wait_ge(masked_ready, n - 1)
                    rows = slice(hh % 2 * HD, (hh % 2 + 1) * HD)
                    for g, at, k0, kn in ((0, 0, 0, SEQ), (1, SEQ, t * P, P), (2, SEQ + P, t * P, P)):
                        last = nc.tensor.matmul(ps[3 + n % 2][:, at:at + kn],
                                                qkT[rows, c % 2, 0, g, hh // 2, t * P:(t + 1) * P],
                                                qkT[rows, c % 2, 1, g, hh // 2, k0:k0 + kn], start=True, stop=True)
                    last.then_inc(scores_ready, 1)

            pe.wait_ge(o_ready, N_STEP)
            turn(1, hn)
            pe.wait_ge(a_lo_ready, 8)
            for n in range(QUARTERS):
                pe.wait_ge(lo_ready, U_WO + n + 1)
                if n >= 2:
                    pe.wait_ge(wo_added, n - 1)
                full_unit(U_WO + n, ps[n % 2])

            pe.wait_ge(hn_ready, 2 * TT)
            turn(2, hn)
            pe.wait_ge(a_lo_ready, 12)
            for s, (kind, b) in enumerate(DENSE_SEQ):
                u = U_DENSE + s
                if (kind == "gate" and b) or s == len(DENSE_SEQ) - 1:
                    d = b - 1 if kind == "gate" else b
                    pe.wait_ge(dh_ready, d + 1)
                    if d:
                        pe.wait_ge(dlo_ready, d)
                    for k in range(2):
                        for t in range(TT):
                            c = k * SEQ + t * P
                            last = nc.tensor.transpose(ps[6][:, c:c + P], dh[:, t, k * P:(k + 1) * P], ident[:, :])
                    last.then_inc(dtr_ready, 1)
                pe.wait_ge(lo_ready, u + 1)
                if kind == "gate":
                    if b:
                        pe.wait_ge(dsilu_ready, b)
                    full_unit(u, ps[4])
                elif kind == "up":
                    if b:
                        pe.wait_ge(dh_ready, b)
                    full_unit(u, ps[5])
                else:
                    pe.wait_ge(dlo_ready, b + 1)
                    for k in range(2):
                        for t in range(TT):
                            for n in range(2):
                                last = product(ps[2 * t + n][:, :], dhT_hi[:, k, t * P:(t + 1) * P],
                                               dhT_lo[:, k, t * P:(t + 1) * P], halves(u, k * D + n * 512, 512),
                                               b == 0 and k == 0, b == N_FB - 1 and k == 1)
                    last.then_inc(unit_used, 1)

            pe.wait_ge(hn_ready, 3 * TT)
            pe.wait_ge(late_landed, 32)
            for k in range(KD):
                for t in range(TT):
                    last = nc.tensor.matmul(ps[4 + k // 2][:, k % 2 * SEQ:(k % 2 + 1) * SEQ], hn[:, t, k * P:(k + 1) * P],
                                            poolmat[:, k // 2, t, :], start=t == 0, stop=t == TT - 1)
                if k % 2:
                    last.then_inc(tr_ready, 1)
            pe.wait_ge(a_lo_ready, 16)
            pe.wait_ge(lo_ready, U_POOL + 1)
            for t in range(TT):
                for g in range(PG):
                    for k in (2 * g, 2 * g + 1):
                        hi, lo = act_of(k, t)
                        last = product(ps[2 * t + g // 2][:, g % 2 * 256:(g % 2 + 1) * 256], hi, lo,
                                       halves(U_POOL, k * 256, 256), k == 2 * g, k == 2 * g + 1)
            last.then_inc(unit_used, 1)

            pe.wait_ge(hn_ready, 4 * TT)
            turn(4, hn)
            pe.wait_ge(hT_ready, 4)
            for t in range(TT):
                for k in range(KD):
                    last = nc.tensor.matmul(ps[0][:, t * E:(t + 1) * E], hT[:, k, t * P:(t + 1) * P], router_sb[:, k, :],
                                            start=k == 0, stop=k == KD - 1)
            last.then_inc(logits_ready, 1)
            pe.wait_ge(sel_ready, 1)
            pe.wait_ge(consts_landed, 16 * 7)
            for t in range(TT):
                for k in range(TT):
                    last = nc.tensor.matmul(ps[1][:, t * E:(t + 1) * E], before[:, k, t * P:(t + 1) * P], route[:, k, 4, :],
                                            start=k == 0, stop=k == TT - 1)
            last.then_inc(prefix_ready, 1)
            pe.wait_ge(over_ready, 1)
            pe.wait_ge(tie_ready, MEMSETS)
            nc.tensor.matmul(ps[2][:, 0:1], ones[:, :], over[:, 0:1], start=True, stop=True).then_inc(overs_summed, 1)

            def gather(g):
                for src, banks in ((a_hi, (3, 5)), (a_lo, (2, 4))):
                    for n in range(2):
                        for q in range(4):
                            for t in range(TT):
                                c = t * D + (4 * n + q) * P
                                last = nc.tensor.matmul(ps[banks[n]][:, q * P:(q + 1) * P], src[:, c:c + P],
                                                        pick[:, t, :], start=t == 0, stop=t == TT - 1)
                        last.then_inc(gather_ready, 1)

            def turn_hidden(i, b):
                pe.wait_ge(h_ready, START + i * N_EB + b + 1)
                pe.wait_ge(hT_lo_ready, START + i * N_EB + b)
                if b == 0:
                    pe.wait_ge(x_added, START + 4 * i)
                for q in range(4):
                    last = nc.tensor.transpose(ps[6][:, q * P:(q + 1) * P], h[:, q * P:(q + 1) * P], ident[:, :])
                last.then_inc(htr_ready, 1)

            def expert(i, last_one):
                at = U_MOE + i * UE
                for j, (kind, b, half) in enumerate(MOE_SEQ):
                    u = U_MOE + j
                    if kind == "gate" and half == 0:
                        if b == 0:
                            pe.wait_ge(xg_hi_ready, 2 * i + 2)
                            pe.wait_ge(xg_lo_ready, 2 * i + 2)
                        elif b == 1:
                            pe.wait_ge(x_added, START + 4 * i)
                        else:
                            pe.wait_ge(h_ready, START + i * N_EB + b - 1)
                    if kind == "down" and half == 0:
                        pe.wait_ge(hT_lo_ready, START + i * N_EB + b + 1)
                        if b == 0:
                            pe.wait_ge(y_lo_ready, START + 2 * i)
                    pe.wait_ge(lo_ready, at + j + 1)
                    if kind == "down":
                        for k in range(2):
                            for n in range(2):
                                first = b == 0 and half == 0 and k == 0
                                final = b == N_EB - 1 and half == 1 and k == 1
                                last = product(ps[n][:, :], hT_hi[:, 2 * half + k, :], hT_lo[:, 2 * half + k, :],
                                               halves(u, k * D + n * 512, 512), first, final)
                    else:
                        bank = ps[(2 if kind == "gate" else 4) + b % 2]
                        for k in range(4):
                            q = 4 * half + k
                            last = product(bank[:, :], xg_hi[:, q, :], xg_lo[:, q, :], halves(u, k * 512, 512),
                                           q == 0, q == KD - 1)
                    last.then_inc(unit_used, 1)
                    if kind == "gate" and half == 0 and b:
                        turn_hidden(i, b - 1)
                    if (kind, b, half) == ("up", 1, 0):
                        pe.wait_ge(x_added, START + 4 * i)
                        for t in range(TT):
                            last = nc.tensor.transpose(ps[7][:, t * P:(t + 1) * P], pick[:, t, :].bitcast(F32), ident[:, :])
                        last.then_inc(place_tr, 1)
                    if (kind, b, half) == ("down", N_EB - 2, 1):
                        turn_hidden(i, N_EB - 1)
                        if not last_one:
                            pe.wait_ge(pick_ready, TT * (i + 2))
                            gather(i + 1)
                pe.wait_ge(place_ready, i + 1)
                for q, (n, t, bank) in enumerate(SCATTER):
                    if t == 0:
                        pe.wait_ge(y_lo_ready, START + 2 * i + n + 1)
                    if q == 2 and not last_one:
                        pe.wait_ge(xg_hi_ready, 2 * i + 4)
                    cols = slice(n * 512, (n + 1) * 512)
                    nc.tensor.matmul(ps[bank][:, :], place[:, t * P:(t + 1) * P], y_hi[:, cols], start=True, stop=False)
                    nc.tensor.matmul(ps[bank][:, :], place[:, t * P:(t + 1) * P], y_lo[:, cols], start=False, stop=True)\
                        .then_inc(scatter_ready, 1)

            def round_of_experts(first):
                pe.wait_ge(pick_ready, TT * (first + 1))
                if first:
                    pe.wait_ge(x_added, START + 4 * first)
                pe.wait_ge(hnsplit_lo, TT)
                gather(first)
                with pe.Fori(0, E - 1) as e:
                    expert(e + first, False)
                expert(first + E - 1, True)

            pe.sem_inc(htr_ready, START)
            round_of_experts(0)
            pe.wait_ge(routed, 1)
            more = pe.value_load(over_i[0:1, 0:1], min_val=0, max_val=1)
            with pe.If(more != 0):
                round_of_experts(E)
                pe.nop()
            with pe.Else():
                pe.nop()


def shape_constants():
    import numpy as np

    order = np.arange(SEQ).reshape(16, 4, 4).transpose(2, 1, 0).reshape(-1)
    dist = order[:, None] - order[None, :]
    near = (dist >= 0) & (dist <= 128)
    by4 = (dist >= 0) & (dist % 4 == 0)
    by16 = (dist >= 0) & (dist % 16 == 0)
    mask = np.empty((TT, P, 4 * P), np.float32)
    for t in range(TT):
        rows = slice(t * P, (t + 1) * P)
        seen = np.concatenate([near[rows], by4[rows, rows], by16[rows, rows]], axis=1)
        mask[t] = np.where(seen, 0.0, MASKED)
    freq = (10000.0 ** (-np.arange(0, HD, 2, dtype=np.float32) / np.float32(HD))).astype(np.float32)
    angle = order[:, None].astype(np.float32) * freq[None, :]
    cos = np.concatenate([np.cos(angle)] * 2, axis=1).astype(np.float32)
    sin = np.concatenate([-np.sin(angle), np.sin(angle)], axis=1).astype(np.float32)
    pool = np.zeros((PG, SEQ, SEQ), np.float32)
    for g, size in enumerate(POOL_SIZES):
        count = np.minimum(order + 1, size).astype(np.float32)
        inside = (dist >= 0) & (dist < size)
        pool[g] = (inside / count[:, None] - np.eye(SEQ)).T
    ident = np.eye(P, dtype=np.float32)
    iota = np.tile(np.arange(SEQ, dtype=np.float32), (P, 1))
    before = np.triu(np.ones((SEQ, SEQ), np.float32), 1)
    return order, dict(mask_in=mask, cos_in=cos, sin_in=sin, ident_in=ident, iota_in=iota,
                       before_in=before, poolmat_in=pool)


INPUTS = ("x", "mix_norm", "ffn_norm", "attn_w_qkv", "attn_w_o", "pool_w", "pool_scale", "dense_w_gate",
          "dense_w_up", "dense_w_down", "moe_router", "moe_w_gate", "moe_w_up", "moe_w_down", "final_norm")


def kernel(**inputs):
    import numpy as np
    import concourse.bacc as bacc
    from concourse import mybir as mb
    from concourse.bass_utils import run_bass_kernel_spmd

    order, constants = shape_constants()
    arrays = {name: np.ascontiguousarray(inputs[name]) for name in INPUTS}
    arrays["x"] = np.ascontiguousarray(arrays["x"][0][order])
    arrays.update(constants)
    nc = bacc.Bacc("TRN2", target_bir_lowering=False, num_devices=1)
    args = [nc.dram_tensor(f"in_{name}", a.shape, mb.dt.from_np(a.dtype), kind="ExternalInput").ap()
            for name, a in arrays.items()]
    args.append(nc.dram_tensor("out_0", (SEQ, D), F32, kind="ExternalOutput").ap())
    program(nc, *args)
    r = run_bass_kernel_spmd(nc, [{f"in_{name}": a for name, a in arrays.items()}], core_ids=[0])
    y = np.empty((1, SEQ, D), np.float32)
    y[0, order] = r.results[0]["out_0"]
    return y
```

```python
from contextlib import ExitStack

import concourse.bass as bass
from concourse import mybir

ALU = mybir.AluOpType
ACT = mybir.ActivationFunctionType
AX = mybir.AxisListType
F32 = mybir.dt.float32
F32R = mybir.dt.float32r
I32 = mybir.dt.int32

P = 128
SEQ = 256
TT = SEQ // P
D = 1024
KD = D // P
GROUPS = 3
HEADS = 16
HD = 64
QW = 256
QUARTERS = D // QW
QH = QW // HD
D_FF = 2816
FB = 256
N_FB = D_FF // FB
E = 8
D_FFE = 3584
EB = 512
N_EB = D_FFE // EB
POOL_SIZES = (2, 4, 8, 16)
PG = len(POOL_SIZES)
EPS = 1e-6
MASKED = -1e30
SCALE = HD ** -0.5

UNIT = 2048
RAW = 4
RING = 11
SPLIT = 3
N_QKV = QUARTERS * GROUPS * 3
U_WO = N_QKV
U_DENSE = U_WO + QUARTERS
U_POOL = U_DENSE + 3 * N_FB
U_MOE = U_POOL + 1
UE = 6 * N_EB
N_STEP = HEADS * TT // 2

DENSE_SEQ = []
for _b in range(N_FB):
    DENSE_SEQ += [("gate", _b), ("up", _b)]
    if _b:
        DENSE_SEQ.append(("down", _b - 1))
DENSE_SEQ.append(("down", N_FB - 1))

MOE_SEQ = []
for _b in range(N_EB):
    MOE_SEQ += [("gate", _b, 0), ("gate", _b, 1), ("up", _b, 0), ("up", _b, 1)]
    if _b:
        MOE_SEQ += [("down", _b - 1, 0), ("down", _b - 1, 1)]
MOE_SEQ += [("down", N_EB - 1, 0), ("down", N_EB - 1, 1)]

EXPERT_SLOT = [_j % RING for _j in range(2 * RING)]
EXPERT_SLOT += [_j % (RING - 1) for _j in range(UE - 2 * RING)]


def ring_uses(j):
    return EXPERT_SLOT[:j].count(EXPERT_SLOT[j]), EXPERT_SLOT.count(EXPERT_SLOT[j])


def slot_before(j):
    n = j - 1
    while EXPERT_SLOT[n % UE] != EXPERT_SLOT[j]:
        n -= 1
    return n


def is_v(u):
    return u % 3 == 2


def qk_index(u):
    return 2 * (u // 3) + u % 3


def pair_of(m):
    return m // 4, m % 4 // 2, m % 2


PIECES = tuple((n, t) for n in range(2) for t in range(TT))

ORDER = []
for _u in range(N_QKV):
    ORDER.append(("unit", _u))
    if _u and not is_v(_u - 1):
        ORDER.append(("turn qk", _u - 1))
    _c, _i = divmod(_u, 3 * GROUPS)
    if _c:
        _m = 4 * (_c - 1) + _i // 2
        if _i % 2:
            ORDER.append(("turn", _m))
        else:
            if _i:
                ORDER.append(("values", _m - 1))
            if _i < 8:
                ORDER.append(("scores", _m))
ORDER += [("turn out", 0), ("scores", 12), ("turn out", 1), ("piece", 0), ("piece", 1), ("split", U_WO + 2),
          ("piece", 2), ("turn", 12), ("scores", 13), ("piece", 3), ("split", U_WO + 3), ("turn out", 2),
          ("values", 12), ("piece", 4), ("turn", 13), ("scores", 14), ("piece", 5), ("values", 13), ("piece", 6),
          ("turn", 14), ("scores", 15), ("piece", 7), ("split", U_WO + 4), ("values", 14), ("piece", 8),
          ("turn", 15), ("piece", 9), ("values", 15), ("piece", 10), ("turn out", 3), ("piece", 11), ("piece", 12),
          ("piece", 13), ("piece", 14), ("turn x", 0), ("piece", 15), ("turn x", 1), ("split", U_WO + 5),
          ("split", U_WO + 6)]

START = 1
CONSTS = 16 * 5

SCATTER = ((0, 0, 7), (0, 1, 6), (1, 0, 3), (1, 1, 5))


def program(nc, x_in, ffn_norm, w_qkv, w_o, pool_w, pool_scale, w_gate, w_up, w_down,
            router, e_gate, e_up, e_down, final_norm, mask_in, cos_in, sin_in, ident_in, iota_in,
            before_in, poolmat_in, inv_count_in,
            gain_col_in, out):
    ctx = ExitStack()
    with ctx:
        def sb(name, shape, dt=F32, scope=ctx):
            return scope.enter_context(nc.sbuf_tensor(name, shape, dt))

        def sem(name):
            return ctx.enter_context(nc.semaphore(name))

        raw = sb("raw", [P, RAW, UNIT])
        w_hi = sb("w_hi", [P, SPLIT, UNIT], F32R)
        w_lo = sb("w_lo", [P, SPLIT, UNIT], F32R)
        a_hi = sb("a_hi", [P, KD * SEQ], F32R)
        a_lo = sb("a_lo", [P, KD * SEQ], F32R)
        x = sb("x", [P, TT, D])
        twin = ExitStack()
        hn = sb("hn", [P, TT, D], F32, twin)
        twin.close()
        hn_hi = sb("hn_hi", [P, TT, D], F32R)
        rows = sb("rows", [P, 3, D])
        gain_col = sb("gain_col", [P, 4, KD])
        ident = sb("ident", [P, P])
        iota = sb("iota", [P, SEQ])
        before = sb("before", [P, TT, SEQ])
        ones = sb("ones", [P, P])
        stat = sb("stat", [P, 5, 8])
        rstat = sb("rstat", [P, 8])
        spare = sb("spare", [P, 4])
        route = sb("route", [P, TT, 8, E])
        posm = sb("posm", [P, TT, E])
        gate_w = sb("gate_w", [P, TT, E])
        rank3 = sb("rank3", [P, 2, TT, E, E])
        inv_count = sb("inv_count", [P, TT, PG])
        tie = sb("tie", [P, E, E])
        over = sb("over", [P, E + 1])
        over_i = sb("over_i", [P, 1], I32)

        attn = ExitStack()
        qkT = sb("qkT", [P, 2, 2, GROUPS, 2, SEQ], F32, attn)
        v_sb = sb("v_sb", [P, 2, GROUPS, TT, QW], F32, attn)
        roped = sb("roped", [P, 2, TT, QW], F32, attn)
        rot = sb("rot", [P, 2, TT, QW], F32, attn)
        s_sb = sb("s_sb", [P, 2, 4 * P], F32, attn)
        e_sb = sb("e_sb", [P, 2, 4 * P], F32, attn)
        eT = sb("eT", [P, 2, 4 * P], F32, attn)
        mask = sb("mask", [P, TT, 4 * P], F32, attn)
        cos = sb("cos", [P, TT, HD], F32, attn)
        sin = sb("sin", [P, TT, HD], F32, attn)
        softs = sb("softs", [P, 2, 4, 2], F32, attn)
        attn.close()

        raw_more = sb("raw_more", [P, 3, UNIT])
        early = ExitStack()
        dh = sb("dh", [P, TT, FB], F32, early)
        dsg = sb("dsg", [P, TT, FB], F32, early)
        dhT_hi = sb("dhT_hi", [P, 2, SEQ], F32R, early)
        dhT_lo = sb("dhT_lo", [P, 2, SEQ], F32R, early)
        twin = ExitStack()
        poolmat_in_f32 = sb("poolmat_in_f32", [P, PG, TT, SEQ], F32, twin)
        twin.close()
        poolmat = sb("poolmat", [P, PG, TT, SEQ], F32R, early)
        hT = sb("hT", [P, KD, SEQ], F32, early)
        early.close()
        raw_late = sb("raw_late", [P, 3, UNIT])
        y_hi = sb("y_hi", [P, D], F32R)
        y_lo = sb("y_lo", [P, D], F32R)
        router_sb = sb("router_sb", [P, KD, E])
        router_g = sb("router_g", [P, KD, E])
        xg_hi = sb("xg_hi", [P, KD, P], F32R)
        xg_lo = sb("xg_lo", [P, KD, P], F32R)
        sg = sb("sg", [P, EB])
        h = sb("h", [P, EB])
        hT_hi = sb("hT_hi", [P, 4, P], F32R)
        hT_lo = sb("hT_lo", [P, 4, P], F32R)
        pick = sb("pick", [P, TT, P], F32R)
        place = sb("place", [P, SEQ], F32R)


        def hidden_T(b):
            if b < N_EB - 1:
                return hT_hi, hT_lo
            return [half[:, 0:EB].rearrange("p (k s) -> p k s", k=4) for half in (y_hi, y_lo)]

        ps = [ctx.enter_context(nc.psum_tensor(f"bank{n}", [P, 512], F32)) for n in range(8)]

        x_landed, ident_landed, tables_landed = sem("x_landed"), sem("ident_landed"), sem("tables_landed")
        gains_landed = sem("gains_landed")
        consts_landed, late_landed = sem("consts_landed"), sem("late_landed")
        raw_landed = [sem(f"raw_landed{n}") for n in range(RAW)]
        ring_landed = [sem(f"ring_landed{n}") for n in range(RING)]
        hi_ready, lo_ready, unit_used = sem("hi_ready"), sem("lo_ready"), sem("unit_used")
        ss_ready, var_ready, std_ready = sem("ss_ready"), sem("var_ready"), sem("std_ready")
        ss1_ready, hT1_ready = sem("ss1_ready"), sem("hT1_ready")
        rstd_ready, hn_ready = sem("rstd_ready"), sem("hn_ready")
        tr_ready, a_hi_ready, a_lo_ready = sem("tr_ready"), sem("a_hi_ready"), sem("a_lo_ready")
        rope_read, rope_ready = sem("rope_read"), sem("rope_ready")
        v_ready, qkT_tr, qkT_ready = sem("v_ready"), sem("qkT_tr"), sem("qkT_ready")
        scores_ready, masked_ready = sem("scores_ready"), sem("masked_ready")
        bias_ready, exp_ready = sem("bias_ready"), sem("exp_ready")
        eT_tr, eT_ready, pv_ready = sem("eT_tr"), sem("eT_ready"), sem("pv_ready")
        rinv_ready, o_ready = sem("rinv_ready"), sem("o_ready")
        o_turned, piece_ready, wo_added = sem("o_turned"), sem("piece_ready"), sem("wo_added")
        router_ready, sqrt_loaded = sem("router_ready"), sem("sqrt_loaded")
        dsilu_ready, dh_ready, dtr_ready = sem("dsilu_ready"), sem("dh_ready"), sem("dtr_ready")
        dhi_ready, dlo_ready, ffn_added = sem("dhi_ready"), sem("dlo_ready"), sem("ffn_added")
        pool_hi_ready, pool_lo_ready, poolmat_ready = sem("pool_hi_ready"), sem("pool_lo_ready"), sem("poolmat_ready")
        pooled, pool_scaled, pool_added = sem("pooled"), sem("pool_scaled"), sem("pool_added")
        hnsplit_hi, hnsplit_lo = sem("hnsplit_hi"), sem("hnsplit_lo")
        hT_ready, logits_ready, route_step = sem("hT_ready"), sem("logits_ready"), sem("route_step")
        shifted_ready, weights_exp = sem("shifted_ready"), sem("weights_exp")
        sel_ready, prefix_ready, over_ready = sem("sel_ready"), sem("prefix_ready"), sem("over_ready")
        overs_summed, routed, tie_ready = sem("overs_summed"), sem("routed"), sem("tie_ready")
        pick_ready, gather_ready = sem("pick_ready"), sem("gather_ready")
        xg_hi_ready, xg_lo_ready = sem("xg_hi_ready"), sem("xg_lo_ready")
        silu_ready, h_ready, htr_ready = sem("silu_ready"), sem("h_ready"), sem("htr_ready")
        hT_hi_ready, hT_lo_ready = sem("hT_hi_ready"), sem("hT_lo_ready")
        place_tr, place_ready = sem("place_tr"), sem("place_ready")
        y_hi_ready, y_lo_ready = sem("y_hi_ready"), sem("y_lo_ready")
        scatter_ready, x_added, out_stored = sem("scatter_ready"), sem("x_added"), sem("out_stored")

        block = ctx.enter_context(nc.Block())

        def unit_source(u):
            if u < U_WO:
                c, g, part = u // 9, u % 9 // 3, u % 3
                n = (g * 3 + part) * D + c * QW
                return w_qkv[0, :, n:n + QW].rearrange("(k p) n -> p k n", p=P)
            if u < U_DENSE:
                n = (u - U_WO) * QW
                return w_o[0, n:n + QW, :].rearrange("(k p) n -> p k n", p=P)
            if u < U_POOL:
                kind, b = DENSE_SEQ[u - U_DENSE]
                if kind == "down":
                    return w_down[0, b * FB:(b + 1) * FB, :].rearrange("(k p) n -> p k n", p=P)
                w = w_gate if kind == "gate" else w_up
                return w[0, :, b * FB:(b + 1) * FB].rearrange("(k p) n -> p k n", p=P)
            return pool_w[0].rearrange("g (k p) n -> p (g k) n", p=P)

        def expert_source(j, e):
            kind, b, half = MOE_SEQ[j]
            if kind == "down":
                r = b * EB + half * 256
                return e_down[0, bass.ds(e, 1), r:r + 256, :].rearrange("a (k p) n -> p (a k) n", p=P)
            w = e_gate if kind == "gate" else e_up
            return w[0, bass.ds(e, 1), half * 512:(half + 1) * 512, b * EB:(b + 1) * EB]\
                .rearrange("a (k p) n -> p (a k) n", p=P)

        ring = [raw_more[:, n, :] for n in range(3)]
        ring += [raw[:, (U_MOE + n) % RAW, :] for n in range(RAW)]
        ring += [raw_late[:, n, :] for n in range(3)]
        ring.append(hn[:, :, :].rearrange("p t d -> p (t d)"))

        def home(u, i=0):
            if u < U_MOE:
                return raw[:, u % RAW, :], raw_landed[u % RAW], 16 * (u // RAW + 1)
            e, j = divmod(u - U_MOE, UE)
            before, uses = ring_uses(j)
            slot = EXPERT_SLOT[j]
            return ring[slot], ring_landed[slot], 16 * (before + 1 + uses * e) + 16 * uses * i

        def split_hi(act, u, i=0):
            where, landed, value = home(u, i)
            act.wait_ge(landed, value)
            if u >= SPLIT:
                act.wait_ge(unit_used, u + 1 - SPLIT + UE * i)
            nc.scalar.activation(w_hi[:, u % SPLIT, :], where, ACT.Copy).then_inc(hi_ready, 1)

        def split_lo(dve, u, i=0):
            dve.wait_ge(hi_ready, u + 1 + UE * i)
            nc.vector.tensor_tensor(w_lo[:, u % SPLIT, :], home(u, i)[0],
                                    w_hi[:, u % SPLIT, :].bitcast(F32), ALU.subtract).then_inc(lo_ready, 1)

        def rstd(m, t):
            return stat[:, m, 6 + t:7 + t]

        def halves(u, at, n):
            return w_hi[:, u % SPLIT, at:at + n], w_lo[:, u % SPLIT, at:at + n]

        def product(bank, hi, lo, w, start, stop):
            nc.tensor.matmul(bank, hi, w[0], start=start, stop=False)
            nc.tensor.matmul(bank, hi, w[1], start=False, stop=False)
            return nc.tensor.matmul(bank, lo, w[0], start=False, stop=stop)

        def act_of(k, t):
            c = slice(k * SEQ + t * P, k * SEQ + (t + 1) * P)
            return a_hi[:, c], a_lo[:, c]

        @block.sync
        def _(sp):
            def load(src, home):
                where, landed, _value = home
                sp.dma_start(where.rearrange("p (k n) -> p k n", k=src.shape[1]), src).then_inc(landed, 16)

            sp.dma_start(ident[:, :], ident_in).then_inc(ident_landed, 16)
            sp.dma_start(x[:, :, :], x_in.rearrange("(t p) d -> p t d", p=P)).then_inc(x_landed, 16)
            for u in range(U_MOE):
                if u >= RAW:
                    sp.wait_ge(lo_ready, u - RAW + 1)
                load(unit_source(u), home(u))

            sp.wait_ge(o_ready, N_STEP)
            late = {7: (unit_used, U_POOL),
                    8: (tr_ready, 12),
                    9: (logits_ready, 1),
                    10: (hnsplit_lo, TT)}
            for j in range(UE):
                if j in late:
                    sp.wait_ge(*late[j])
                elif j >= RING:
                    sp.wait_ge(lo_ready, U_MOE + slot_before(j) + 1)
                elif j >= 3:
                    sp.wait_ge(lo_ready, U_MOE - RAW + j - 3 + 1)
                load(expert_source(j, 0), home(U_MOE + j))

            def expert(i, e):
                for j in range(UE):
                    sp.wait_ge(lo_ready, U_MOE + slot_before(j) + 1 + i * UE)
                    load(expert_source(j, e), home(U_MOE + j, i))

            with sp.Fori(1, E) as e:
                expert(e, e)
            sp.wait_ge(routed, 1)
            more = sp.value_load(over_i[0:1, 0:1], min_val=0, max_val=1)
            with sp.If(more != 0):
                with sp.Fori(0, E) as e:
                    expert(e + E, e)
            with sp.Else():
                sp.nop()
            for t in range(TT):
                sp.wait_ge(hn_ready, TT + t + 1)
                sp.dma_start(out[t * P:(t + 1) * P, :], hn[:, t, :]).then_inc(out_stored, 16)
            sp.wait_ge(out_stored, 16 * TT)

        @block.gpsimd
        def _(pool):
            nc.gpsimd.memset(spare[:, 0:1], 1.0).then_inc(tie_ready, 1)
            nc.gpsimd.memset(ones[:, :], 1.0).then_inc(tie_ready, 1)
            for e in range(E):
                if e:
                    nc.gpsimd.memset(tie[:, e, 0:e], 1.0).then_inc(tie_ready, 1)
                nc.gpsimd.memset(tie[:, e, e:E], 0.0).then_inc(tie_ready, 1)
            for n in range(N_QKV * 2 // 3):
                pool.wait_ge(rope_read, n + 1)
                nc.gpsimd.tensor_tensor(roped[:, n % 2], roped[:, n % 2], rot[:, n % 2], ALU.add)\
                    .then_inc(rope_ready, 1)

            pool.wait_ge(o_ready, N_STEP)
            pool.dma_start(poolmat_in_f32[:, :, :, :].rearrange("p g t n -> p (g t) n"),
                           poolmat_in.rearrange("g (t p) n -> p (g t) n", p=P)).then_inc(late_landed, 16)
            pool.dma_start(inv_count[:, :, :], inv_count_in.rearrange("(t p) g -> p t g", p=P)).then_inc(late_landed, 16)
            pool.dma_start(router_sb[:, :, :], router[0].rearrange("(k p) e -> p k e", p=P)).then_inc(late_landed, 16)

            for t in range(TT):
                pool.wait_ge(hnsplit_hi, t + 1)
                nc.gpsimd.tensor_tensor(a_lo[:, t * D:(t + 1) * D], hn[:, t, :], a_hi[:, t * D:(t + 1) * D].bitcast(F32),
                                        ALU.subtract).then_inc(hnsplit_lo, 1)

        MEMSETS = 2 * E + 1

        @block.scalar
        def _(act):
            act.dma_start(gain_col[:, :, :], gain_col_in.rearrange("p (m k) -> p m k", m=4)).then_inc(gains_landed, 16)
            def load_table(func, n=0):
                nc.scalar.activation(spare[:, 1 + n:2 + n], spare[:, 0:1], func)

            def squares(m):
                nc.scalar.activation(hn[:, 0, :], x[:, 0, :], ACT.Square, accum_out=stat[:, m, 0:1]).then_inc(ss_ready, 1)

            def root(m):
                act.wait_ge(var_ready, m + 1)
                nc.scalar.activation(stat[:, m, 4:4 + TT], stat[:, m, 2:2 + TT], ACT.Sqrt).then_inc(std_ready, 1)

            def split_turned(m, k):
                src = ps[4 + k // 2][:, k % 2 * SEQ:(k % 2 + 1) * SEQ]
                dst = a_hi[:, k * SEQ:(k + 1) * SEQ]
                nc.scalar.activation(dst, src, ACT.Copy, scale=gain_col[:, m, k:k + 1]).then_inc(a_hi_ready, 1)

            def split_all(m, turns):
                for k in range(KD):
                    if k % 2 == 0:
                        act.wait_ge(tr_ready, turns + k // 2 + 1)
                    split_turned(m, k)

            act.wait_ge(tie_ready, 1)
            load_table(ACT.Copy)
            act.wait_ge(gains_landed, 16)
            act.wait_ge(x_landed, 16)
            split_all(0, 0)
            for dst, src in ((cos[:, :, :], cos_in.rearrange("(t p) d -> p t d", p=P)),
                             (sin[:, :, :], sin_in.rearrange("(t p) d -> p t d", p=P)),
                             (mask[:, :, :], mask_in.rearrange("t p d -> p t d"))):
                act.dma_start(dst, src).then_inc(tables_landed, 16)
            split_hi(act, 0)
            split_hi(act, 1)
            squares(0)
            root(0)
            for dst, src in ((iota[:, :], iota_in),
                             (before[:, :, :], before_in.rearrange("(t p) d -> p t d", p=P)),
                             (rows[:, 0, :], pool_scale[0:1, :].to_broadcast([P, D])),
                             (rows[:, 1, :], ffn_norm[1:2, :].to_broadcast([P, D])),
                             (rows[:, 2, :], final_norm.rearrange("(a n) -> a n", a=1).to_broadcast([P, D]))):
                act.dma_start(dst, src).then_inc(consts_landed, 16)

            def output_halves(c):
                act.wait_ge(o_turned, c + 1)
                nc.scalar.activation(a_hi[:, c * 512:(c + 1) * 512], ps[2][:, :], ACT.Copy).then_inc(a_hi_ready, 1)

            split_hi(act, 2)
            act.wait_ge(rstd_ready, 1)
            for kind, n in ORDER:
                if kind == "unit":
                    act.wait_ge(unit_used, n + 1)
                    if is_v(n):
                        g, c = n % 9 // 3, n // 9
                        if c >= 2:
                            act.wait_ge(pv_ready, 4 * (c - 1))
                        for t in range(TT):
                            last = nc.scalar.activation(v_sb[:, c % 2, g, t], ps[n % 2][:, t * QW:(t + 1) * QW],
                                                        ACT.Copy, scale=rstd(0, t))
                        last.then_inc(v_ready, 1)
                    if n < N_QKV - 1:
                        split_hi(act, n + 3)
                elif kind == "turn qk":
                    g, c = n % 9 // 3, n // 9
                    act.wait_ge(qkT_tr, qk_index(n) + 1)
                    if c >= 2:
                        act.wait_ge(scores_ready, 4 * (c - 1))
                    nc.scalar.activation(qkT[:, c % 2, n % 3, g].rearrange("p a t -> p (a t)"), ps[2][:, :],
                                         ACT.Copy).then_inc(qkT_ready, 1)
                elif kind == "scores":
                    for side in range(2):
                        act.wait_ge(bias_ready, 2 * n + side + 1)
                        if n:
                            act.wait_ge(eT_tr, n)
                        if n >= 2:
                            act.wait_ge(rinv_ready, n - 1)
                        nc.scalar.activation(e_sb[:, side, :], s_sb[:, side, :], ACT.Exp, scale=SCALE,
                                             bias=softs[:, n % 2, 1, side:side + 1],
                                             accum_out=softs[:, n % 2, 2, side:side + 1]).then_inc(exp_ready, 1)
                elif kind == "turn":
                    act.wait_ge(eT_tr, n + 1)
                    if n:
                        act.wait_ge(pv_ready, n)
                    for side in range(2):
                        nc.scalar.activation(eT[:, side, :], ps[5 + side][:, :], ACT.Copy).then_inc(eT_ready, 1)
                elif kind == "turn out":
                    output_halves(n)
                elif kind == "split":
                    split_hi(act, n)
                elif kind == "turn x":
                    for j in (2 * n, 2 * n + 1):
                        act.wait_ge(tr_ready, 4 + j + 1)
                        split_turned(1, 2 * j)
                        split_turned(1, 2 * j + 1)
            act.wait_ge(wo_added, 4 * QUARTERS)
            squares(1)
            root(1)
            act.wait_ge(rstd_ready, 2)

            for s, (kind, b) in enumerate(DENSE_SEQ):
                if kind == "up":
                    act.wait_ge(unit_used, U_DENSE + s)
                    if b:
                        act.wait_ge(dh_ready, b)
                    for t in range(TT):
                        last = nc.scalar.activation(dsg[:, t, :], ps[4][:, t * FB:(t + 1) * FB], ACT.Silu,
                                                    scale=rstd(1, t))
                    last.then_inc(dsilu_ready, 1)
                if (kind == "gate" and b) or s == len(DENSE_SEQ) - 1:
                    d = b - 1 if kind == "gate" else b
                    act.wait_ge(dtr_ready, d + 1)
                    nc.scalar.activation(dhT_hi[:, :, :], ps[6][:, :].rearrange("p (k t) -> p k t", k=2), ACT.Copy)\
                        .then_inc(dhi_ready, 1)
                if s and U_DENSE + s + 2 < U_MOE:
                    split_hi(act, U_DENSE + s + 2)
                if s == N_FB:
                    act.wait_ge(late_landed, 48)
                    nc.scalar.activation(poolmat[:, :, :, :], poolmat_in_f32[:, :, :, :], ACT.Copy)\
                        .then_inc(poolmat_ready, 1)
            split_hi(act, U_MOE)

            load_table(ACT.Sqrt, 0)
            act.wait_ge(ffn_added, 2)
            squares(2)
            root(2)
            act.wait_ge(rstd_ready, 3)
            for t in range(TT):
                nc.scalar.activation(hn_hi[:, t, :], x[:, t, :], ACT.Copy, scale=rstd(2, t))\
                    .then_inc(pool_hi_ready, 1)
            split_all(2, 8)
            split_hi(act, U_MOE + 1)

            for j in (0, 2):
                act.wait_ge(tr_ready, 12 + j + 1)
                nc.scalar.activation(hT[:, 2 * j:2 * j + 2, :], ps[4 + j][:, :].rearrange("p (k t) -> p k t", k=2),
                                     ACT.Copy).then_inc(hT_ready, 1)
            act.wait_ge(pool_added, 4)
            squares(3)
            root(3)
            load_table(ACT.Exp, 1)
            split_hi(act, U_MOE + 2)
            for t in range(TT):
                act.wait_ge(hn_ready, t + 1)
                nc.scalar.activation(a_hi[:, t * D:(t + 1) * D], hn[:, t, :], ACT.Copy).then_inc(hnsplit_hi, 1)
            act.wait_ge(shifted_ready, 1)
            nc.scalar.activation(route[:, :, 2, :], route[:, :, 1, :], ACT.Exp).then_inc(weights_exp, 1)

            def gather(g):
                for n in range(2):
                    act.wait_ge(gather_ready, 4 * g + 2 * n + 1)
                    nc.scalar.activation(xg_hi[:, 4 * n:4 * n + 4, :],
                                         ps[(3, 5)[n]][:, :].rearrange("p (k s) -> p k s", k=4), ACT.Copy)\
                        .then_inc(xg_hi_ready, 1)

            def expert(i, last):
                at = U_MOE + i * UE
                load_table(ACT.Silu, 1)
                for j, (kind, b, half) in enumerate(MOE_SEQ):
                    if kind == "up" and half == 0:
                        act.wait_ge(unit_used, at + j)
                        act.wait_ge(h_ready, START + i * N_EB + b)
                        nc.scalar.activation(sg[:, :], ps[2 + b % 2][:, :], ACT.Silu).then_inc(silu_ready, 1)
                    if half == 1 and (kind == "gate" and b or kind == "down" and b == N_EB - 2):
                        d = b - 1 if kind == "gate" else b + 1
                        act.wait_ge(htr_ready, START + i * N_EB + d + 1)
                        nc.scalar.activation(hidden_T(d)[0][:, :, :], ps[6][:, :].rearrange("p (k s) -> p k s", k=4), ACT.Copy)\
                            .then_inc(hT_hi_ready, 1)
                    if (kind, b, half) == ("up", 1, 1):
                        act.wait_ge(place_tr, i + 1)
                        nc.scalar.activation(place[:, :], ps[7][:, 0:SEQ], ACT.Copy).then_inc(place_ready, 1)
                    if j and (j + 2 < UE or not last):
                        split_hi(act, U_MOE + j + 2, i)
                act.wait_ge(unit_used, at + UE)
                for n in range(2):
                    nc.scalar.activation(y_hi[:, n * 512:(n + 1) * 512], ps[n][:, :], ACT.Copy)\
                        .then_inc(y_hi_ready, 1)
                if not last:
                    gather(i + 1)
                    split_hi(act, U_MOE + UE + 2, i)

            def round_of_experts(first):
                gather(first)
                with act.Fori(0, E - 1) as e:
                    expert(e + first, False)
                expert(first + E - 1, True)
                load_table(ACT.Sqrt, 2 if first else 0)
                act.wait_ge(x_added, START + 4 * (first + E))

            round_of_experts(0)
            act.wait_ge(routed, 1)
            more = act.value_load(over_i[0:1, 0:1], min_val=0, max_val=1)
            with act.If(more != 0):
                split_hi(act, U_MOE + E * UE)
                split_hi(act, U_MOE + E * UE + 1)
                split_hi(act, U_MOE + E * UE + 2)
                round_of_experts(E)
                act.nop()
            with act.Else():
                act.nop()
            squares(4)
            root(4)

        @block.vector
        def _(dve):
            dve.wait_ge(tie_ready, MEMSETS)

            def squares(m):
                nc.vector.tensor_tensor_reduce(out=hn[:, 1, :], in0=x[:, 1, :], in1=x[:, 1, :], scale=1.0, scalar=0.0,
                                               op0=ALU.mult, op1=ALU.add, accum_out=stat[:, m, 1:2])\
                    .then_inc(ss1_ready, 1)

            def mean(m):
                dve.wait_ge(ss1_ready, m + 1)
                dve.wait_ge(ss_ready, m + 1)
                nc.vector.tensor_scalar(stat[:, m, 2:2 + TT], stat[:, m, 0:TT], 1.0 / D, EPS, ALU.mult, ALU.add)\
                    .then_inc(var_ready, 1)

            def invert(m):
                dve.wait_ge(std_ready, m + 1)
                nc.vector.reciprocal(stat[:, m, 6:6 + TT], stat[:, m, 4:4 + TT]).then_inc(rstd_ready, 1)
                dve.wait_ge(rstd_ready, m + 1)

            def normed(m, row):
                for t in range(TT):
                    nc.vector.scalar_tensor_tensor(hn[:, t, :], x[:, t, :], rstd(m, t), rows[:, row, :],
                                                   ALU.mult, ALU.mult).then_inc(hn_ready, 1)

            def split_turned(m, before_these, tiles):
                for k in tiles:
                    if k % 2 == 0:
                        dve.wait_ge(a_hi_ready, before_these + k + 2)
                    cols = slice(k * SEQ, (k + 1) * SEQ)
                    nc.vector.scalar_tensor_tensor(a_lo[:, cols], ps[4 + k // 2][:, k % 2 * SEQ:(k % 2 + 1) * SEQ],
                                                   gain_col[:, m, k:k + 1], a_hi[:, cols].bitcast(F32),
                                                   ALU.mult, ALU.subtract).then_inc(a_lo_ready, 1)

            def split_all(m, before_these):
                split_turned(m, before_these, range(KD))

            def output_halves(c):
                dve.wait_ge(a_hi_ready, KD + c + 1)
                cols = slice(c * 512, (c + 1) * 512)
                nc.vector.tensor_tensor(a_lo[:, cols], ps[2][:, :], a_hi[:, cols].bitcast(F32), ALU.subtract)\
                    .then_inc(a_lo_ready, 1)

            def add_piece(q):
                n, t = PIECES[q % 4]
                if q % 4 == 3:
                    dve.wait_ge(unit_used, U_WO + q // 4 + 1)
                else:
                    dve.wait_ge(piece_ready, 3 * (q // 4) + q % 4 + 1)
                cols = x[:, t, n * 512:(n + 1) * 512]
                nc.vector.tensor_tensor(cols, cols, ps[q % 2][:, :], ALU.add).then_inc(wo_added, 1)

            dve.wait_ge(gains_landed, 16)
            split_all(0, 0)
            split_lo(dve, 0)
            split_lo(dve, 1)
            dve.wait_ge(x_landed, 16)
            squares(0)
            mean(0)
            invert(0)
            dve.wait_ge(tables_landed, 16 * 3)

            split_lo(dve, 2)
            for kind, n in ORDER:
                if kind == "unit":
                    if not is_v(n):
                        q = qk_index(n)
                        dve.wait_ge(unit_used, n + 1)
                        if q >= 2:
                            dve.wait_ge(qkT_tr, q - 1)
                            dve.wait_ge(rope_ready, q - 1)
                        bank = ps[n % 2][:, :].rearrange("p (t a n) -> p t a n", t=TT, a=QH)
                        dst = roped[:, q % 2].rearrange("p t (a n) -> p t a n", a=QH)
                        turned = rot[:, q % 2].rearrange("p t (a n) -> p t a n", a=QH)
                        h2 = HD // 2
                        for t in range(TT):
                            nc.vector.scalar_tensor_tensor(dst[:, t], bank[:, t], rstd(0, t),
                                                           cos[:, t, :].unsqueeze(1).to_broadcast([P, QH, HD]),
                                                           ALU.mult, ALU.mult)
                            for lo, hi in ((0, h2), (h2, 0)):
                                last = nc.vector.scalar_tensor_tensor(
                                    turned[:, t, :, lo:lo + h2], bank[:, t, :, hi:hi + h2], rstd(0, t),
                                    sin[:, t, lo:lo + h2].unsqueeze(1).to_broadcast([P, QH, h2]), ALU.mult, ALU.mult)
                        last.then_inc(rope_read, 1)
                    if n < N_QKV - 1:
                        split_lo(dve, n + 3)
                elif kind == "scores":
                    t = pair_of(n)[2]
                    dve.wait_ge(scores_ready, n + 1)
                    for side in range(2):
                        if n:
                            dve.wait_ge(exp_ready, 2 * n + side - 1)
                        if n >= 2:
                            dve.wait_ge(o_ready, n - 1)
                        nc.vector.tensor_tensor_reduce(out=s_sb[:, side, :], in0=ps[3 + side][:, :], in1=mask[:, t, :],
                                                       scale=1.0, scalar=-3e38, op0=ALU.add, op1=ALU.max,
                                                       accum_out=softs[:, n % 2, 0, side:side + 1])\
                            .then_inc(masked_ready, 1)
                        dve.wait_ge(masked_ready, 2 * n + side + 1)
                        nc.vector.tensor_scalar(softs[:, n % 2, 1, side:side + 1], softs[:, n % 2, 0, side:side + 1],
                                                -SCALE, None, ALU.mult).then_inc(bias_ready, 1)
                elif kind == "values":
                    c, pair, t = pair_of(n)
                    at = (c * QH + 2 * pair) * HD
                    dve.wait_ge(exp_ready, 2 * n + 2)
                    nc.vector.reciprocal(softs[:, n % 2, 3, :], softs[:, n % 2, 2, :]).then_inc(rinv_ready, 1)
                    dve.wait_ge(rinv_ready, n + 1)
                    dve.wait_ge(pv_ready, n + 1)
                    nc.vector.tensor_tensor(hn[:, t, at:at + 2 * HD].rearrange("p (a n) -> p a n", a=2),
                                            ps[7][:, 0:2 * HD].rearrange("p (a n) -> p a n", a=2),
                                            softs[:, n % 2, 3, :].unsqueeze(2).to_broadcast([P, 2, HD]), ALU.mult)\
                        .then_inc(o_ready, 1)
                elif kind == "turn out":
                    output_halves(n)
                elif kind == "piece":
                    add_piece(n)
                elif kind == "split":
                    split_lo(dve, n)
                elif kind == "turn x" and n:
                    split_all(1, KD + QUARTERS)
            dve.wait_ge(wo_added, 4 * QUARTERS)
            squares(1)
            mean(1)
            invert(1)

            for s, (kind, b) in enumerate(DENSE_SEQ):
                if s and DENSE_SEQ[s - 1][0] == "up":
                    d = DENSE_SEQ[s - 1][1]
                    dve.wait_ge(unit_used, U_DENSE + s)
                    dve.wait_ge(dsilu_ready, d + 1)
                    if d:
                        dve.wait_ge(dtr_ready, d)
                    for t in range(TT):
                        last = nc.vector.scalar_tensor_tensor(dh[:, t, :], ps[5][:, t * FB:(t + 1) * FB], rstd(1, t),
                                                              dsg[:, t, :], ALU.mult, ALU.mult)
                    last.then_inc(dh_ready, 1)
                    if d == 0:
                        split_lo(dve, U_DENSE + 3)
                if (kind == "gate" and b) or s == len(DENSE_SEQ) - 1:
                    d = b - 1 if kind == "gate" else b
                    dve.wait_ge(dhi_ready, d + 1)
                    nc.vector.tensor_tensor(dhT_lo[:, :, :], ps[6][:, :].rearrange("p (k t) -> p k t", k=2),
                                            dhT_hi[:, :, :].bitcast(F32), ALU.subtract).then_inc(dlo_ready, 1)
                if s > 1 and U_DENSE + s + 2 < U_MOE:
                    split_lo(dve, U_DENSE + s + 2)
            split_lo(dve, U_MOE)
            dve.wait_ge(unit_used, U_POOL)
            for t in range(TT):
                for n in range(2):
                    cols = x[:, t, n * 512:(n + 1) * 512]
                    nc.vector.tensor_tensor(cols, cols, ps[2 * t + n][:, :], ALU.add).then_inc(ffn_added, 1)
            dve.wait_ge(ffn_added, 4)
            squares(2)
            mean(2)
            invert(2)
            for t in range(TT):
                dve.wait_ge(pool_hi_ready, t + 1)
                nc.vector.scalar_tensor_tensor((y_hi, y_lo)[t][:, :], x[:, t, :], rstd(2, t), hn_hi[:, t, :].bitcast(F32),
                                               ALU.mult, ALU.subtract).then_inc(pool_lo_ready, 1)
            dve.wait_ge(late_landed, 48)
            nc.vector.tensor_tensor(router_g[:, :, :], router_sb[:, :, :],
                                    gain_col[:, 3, :].unsqueeze(2).to_broadcast([P, KD, E]), ALU.mult)\
                .then_inc(router_ready, 1)
            split_all(2, 2 * KD + QUARTERS)

            dve.wait_ge(consts_landed, CONSTS)
            for q, (n, t) in enumerate(PIECES):
                if n == 0:
                    dve.wait_ge(pooled, 1)
                else:
                    dve.wait_ge(unit_used, U_POOL + 1)
                for g in (2 * n, 2 * n + 1):
                    c = slice(g * 256, (g + 1) * 256)
                    last = nc.vector.scalar_tensor_tensor(hn[:, t, c], ps[2 * t + n][:, g % 2 * 256:(g % 2 + 1) * 256],
                                                          inv_count[:, t, g:g + 1], rows[:, 0, c], ALU.mult, ALU.mult)
                last.then_inc(pool_scaled, 1)
                dve.wait_ge(pool_scaled, q + 1)
                cols = slice(n * 512, (n + 1) * 512)
                nc.vector.tensor_tensor(x[:, t, cols], x[:, t, cols], hn[:, t, cols], ALU.add)\
                    .then_inc(pool_added, 1)
            for n, j in enumerate((1, 3)):
                dve.wait_ge(tr_ready, 12 + j + 1)
                nc.vector.tensor_copy(hT[:, 2 * j:2 * j + 2, :], ps[4 + j][:, :].rearrange("p (k t) -> p k t", k=2))\
                    .then_inc(hT1_ready, 1)
            dve.wait_ge(pool_added, 4)
            squares(3)
            mean(3)
            invert(3)
            normed(3, 1)

            steps = [0]

            def chain(instruction):
                steps[0] += 1
                instruction.then_inc(route_step, 1)
                dve.wait_ge(route_step, steps[0])

            dve.wait_ge(logits_ready, 1)
            lg, shifted, ex, rank, sel, wt, pos, far = (route[:, :, n, :] for n in range(8))
            nc.vector.tensor_scalar(lg[:, 0], ps[0][:, 0:E], rstd(3, 0), None, ALU.mult)
            chain(nc.vector.tensor_scalar(lg[:, 1], ps[2][:, 0:E], rstd(3, 1), None, ALU.mult))
            chain(nc.vector.tensor_reduce(rstat[:, 0:TT], lg, AX.X, ALU.max))
            nc.vector.tensor_tensor(shifted, lg, rstat[:, 0:TT].unsqueeze(2).to_broadcast([P, TT, E]), ALU.subtract)\
                .then_inc(shifted_ready, 1)
            other = lg.unsqueeze(2).to_broadcast([P, TT, E, E])
            own = lg.unsqueeze(3).to_broadcast([P, TT, E, E])
            chain(nc.vector.tensor_tensor(rank3[:, 1], other, own, ALU.is_equal))
            chain(nc.vector.tensor_tensor(rank3[:, 1], rank3[:, 1], tie[:, :, :].unsqueeze(1).to_broadcast([P, TT, E, E]),
                                          ALU.mult))
            chain(nc.vector.tensor_tensor(rank3[:, 0], other, own, ALU.is_gt))
            chain(nc.vector.tensor_tensor(rank3[:, 0], rank3[:, 0], rank3[:, 1], ALU.add))
            chain(nc.vector.tensor_reduce(rank, rank3[:, 0], AX.X, ALU.add))
            nc.vector.tensor_scalar(sel, rank, 2.0, None, ALU.is_lt).then_inc(sel_ready, 1)
            dve.wait_ge(sel_ready, 1)
            dve.wait_ge(weights_exp, 1)
            chain(nc.vector.tensor_tensor(wt, ex, sel, ALU.mult))
            chain(nc.vector.tensor_reduce(rstat[:, 2:2 + TT], wt, AX.X, ALU.add))
            chain(nc.vector.reciprocal(rstat[:, 4:4 + TT], rstat[:, 2:2 + TT]))
            chain(nc.vector.tensor_tensor(gate_w[:, :, :], wt, rstat[:, 4:4 + TT].unsqueeze(2).to_broadcast([P, TT, E]),
                                          ALU.mult))
            dve.wait_ge(prefix_ready, 1)
            chain(nc.vector.scalar_tensor_tensor(pos, ps[1][:, 0:TT * E].rearrange("p (t e) -> p t e", t=TT), 1.0,
                                                 sel, ALU.add, ALU.mult))
            chain(nc.vector.tensor_scalar(posm[:, :, :], pos, -1.0, None, ALU.add))
            def pick_slots(i, first):
                shift = 0 if first == 0 else P
                for t in range(TT):
                    nc.vector.tensor_scalar(pick[:, t, :], iota[:, shift:shift + P], posm[:, t, bass.ds(i - first, 1)],
                                            None, ALU.is_equal).then_inc(pick_ready, 1)

            def gather(g):
                for n in range(2):
                    dve.wait_ge(gather_ready, 4 * g + 2 * n + 2)
                    nc.vector.tensor_copy(xg_lo[:, 4 * n:4 * n + 4, :],
                                          ps[(2, 4)[n]][:, :].rearrange("p (k s) -> p k s", k=4)).then_inc(xg_lo_ready, 1)

            def expert(i, first, last):
                at = U_MOE + i * UE
                for j, (kind, b, half) in enumerate(MOE_SEQ):
                    if j and MOE_SEQ[j - 1][0] == "up" and MOE_SEQ[j - 1][2] == 1:
                        d = MOE_SEQ[j - 1][1] + i * N_EB
                        dve.wait_ge(unit_used, at + j)
                        dve.wait_ge(silu_ready, d + 1)
                        dve.wait_ge(htr_ready, START + d)
                        nc.vector.tensor_tensor(h[:, :], sg[:, :], ps[4 + MOE_SEQ[j - 1][1] % 2][:, :], ALU.mult)\
                            .then_inc(h_ready, 1)
                    if half == 1 and (kind == "gate" and b or kind == "down" and b == N_EB - 2):
                        d = b - 1 if kind == "gate" else b + 1
                        dve.wait_ge(hT_hi_ready, i * N_EB + d + 1)
                        h_hi, h_lo = hidden_T(d)
                        nc.vector.tensor_tensor(h_lo[:, :, :], ps[6][:, :].rearrange("p (k s) -> p k s", k=4),
                                                h_hi[:, :, :].bitcast(F32), ALU.subtract).then_inc(hT_lo_ready, 1)
                    if (kind, b, half) == ("gate", 3, 0) and not last:
                        dve.wait_ge(place_tr, i + 1)
                        pick_slots(i + 1, first)
                    if j and (j + 2 < UE or not last):
                        split_lo(dve, U_MOE + j + 2, i)
                for n in range(2):
                    dve.wait_ge(y_hi_ready, 2 * i + n + 1)
                    cols = slice(n * 512, (n + 1) * 512)
                    nc.vector.tensor_tensor(y_lo[:, cols], ps[n][:, :], y_hi[:, cols].bitcast(F32), ALU.subtract)\
                        .then_inc(y_lo_ready, 1)
                if not last:
                    gather(i + 1)
                for q, (n, t, bank) in enumerate(SCATTER):
                    dve.wait_ge(scatter_ready, 4 * i + q + 1)
                    cols = x[:, t, n * 512:(n + 1) * 512]
                    nc.vector.scalar_tensor_tensor(cols, ps[bank][:, :], gate_w[:, t, bass.ds(i - first, 1)], cols,
                                                   ALU.mult, ALU.add).then_inc(x_added, 1)
                if not last:
                    split_lo(dve, U_MOE + UE + 2, i)

            def round_of_experts(first):
                if first:
                    pick_slots(first, first)
                else:
                    split_lo(dve, U_MOE + 1)
                gather(first)
                if not first:
                    split_lo(dve, U_MOE + 2)
                if not first:
                    dve.wait_ge(overs_summed, 1)
                    nc.vector.tensor_scalar(over_i[:, :], ps[7][:, 0:1], 1.0, None, ALU.min).then_inc(routed, 1)
                with dve.Fori(0, E - 1) as e:
                    expert(e + first, first, False)
                expert(first + E - 1, first, True)
                dve.wait_ge(x_added, START + 4 * (first + E))

            for counter in (h_ready, hT_lo_ready, x_added, y_lo_ready):
                dve.sem_inc(counter, START)
            pick_slots(0, 0)
            chain(nc.vector.tensor_scalar(far, posm[:, :, :], float(P), None, ALU.is_ge))
            nc.vector.tensor_reduce(over[:, 0:1], far, AX.XY, ALU.add).then_inc(over_ready, 1)
            round_of_experts(0)
            more = dve.value_load(over_i[0:1, 0:1], min_val=0, max_val=1)
            with dve.If(more != 0):
                split_lo(dve, U_MOE + E * UE)
                split_lo(dve, U_MOE + E * UE + 1)
                split_lo(dve, U_MOE + E * UE + 2)
                round_of_experts(E)
                dve.nop()
            with dve.Else():
                dve.nop()
            squares(4)
            mean(4)
            invert(4)
            normed(4, 2)

        @block.tensor
        def _(pe):
            def turn(src, j):
                for k in range(2):
                    for t in range(TT):
                        c = (2 * j + k) * P
                        last = nc.tensor.transpose(ps[4 + j][:, k * SEQ + t * P:k * SEQ + (t + 1) * P],
                                                   src[:, t, c:c + P], ident[:, :])
                last.then_inc(tr_ready, 1)

            def turn_output(c):
                if c:
                    pe.wait_ge(a_lo_ready, KD + c)
                for k in range(2):
                    for t in range(TT):
                        last = nc.tensor.transpose(ps[2][:, k * SEQ + t * P:k * SEQ + (t + 1) * P],
                                                   hn[:, t, (2 * c + k) * P:(2 * c + k + 1) * P], ident[:, :])
                last.then_inc(o_turned, 1)

            def project(q):
                c, (n, t) = q // 4, PIECES[q % 4]
                pe.wait_ge(a_lo_ready, KD + c + 1)
                pe.wait_ge(lo_ready, U_WO + c + 1)
                if q >= 2:
                    pe.wait_ge(wo_added, q - 1)
                elif q == 0:
                    pe.wait_ge(rope_read, qk_index(N_QKV - 2) + 1)
                else:
                    pe.wait_ge(v_ready, N_QKV // 3)
                for k in range(2):
                    hi, lo = act_of(2 * c + k, t)
                    last = product(ps[q % 2][:, :], hi, lo, halves(U_WO + c, k * D + n * 512, 512), k == 0, k == 1)
                last.then_inc(unit_used if q % 4 == 3 else piece_ready, 1)

            def full_unit(u, bank, before=None):
                for t in range(TT):
                    for k in range(KD):
                        if before is not None and t == 0 and k % 2 == 0:
                            pe.wait_ge(a_lo_ready, before + k + 2)
                        hi, lo = act_of(k, t)
                        last = product(bank[:, t * QW:(t + 1) * QW], hi, lo, halves(u, k * QW, QW), k == 0, k == KD - 1)
                last.then_inc(unit_used, 1)

            pe.wait_ge(ident_landed, 16)
            pe.wait_ge(x_landed, 16)
            for j in range(4):
                turn(x, j)

            for kind, n in ORDER:
                if kind == "unit":
                    pe.wait_ge(lo_ready, n + 1)
                    if n >= 2 and is_v(n - 2):
                        pe.wait_ge(v_ready, (n - 2) // 3 + 1)
                    elif n >= 2:
                        pe.wait_ge(rope_read, qk_index(n - 2) + 1)
                    full_unit(n, ps[n % 2], None if n else 0)
                elif kind == "turn qk":
                    q = qk_index(n)
                    pe.wait_ge(rope_ready, q + 1)
                    if q:
                        pe.wait_ge(qkT_ready, q)
                    for pair in range(2):
                        for t in range(TT):
                            c = pair * SEQ + t * P
                            last = nc.tensor.transpose(ps[2][:, c:c + P], roped[:, q % 2, t, pair * P:(pair + 1) * P],
                                                       ident[:, :])
                    last.then_inc(qkT_tr, 1)
                elif kind == "scores":
                    c, pair, t = pair_of(n)
                    if n % 4 == 0:
                        pe.wait_ge(qkT_ready, 2 * GROUPS * (c + 1))
                    if n:
                        pe.wait_ge(masked_ready, 2 * n)
                    for g, at, k0, kn in ((0, 0, 0, SEQ), (1, SEQ, t * P, P), (2, SEQ + P, t * P, P)):
                        for side in range(2):
                            part = slice(side * HD, (side + 1) * HD)
                            last = nc.tensor.matmul(ps[3 + side][:, at:at + kn],
                                                    qkT[part, c % 2, 0, g, pair, t * P:(t + 1) * P],
                                                    qkT[part, c % 2, 1, g, pair, k0:k0 + kn], start=True, stop=True)
                    last.then_inc(scores_ready, 1)
                elif kind == "turn":
                    for side in range(2):
                        pe.wait_ge(exp_ready, 2 * n + side + 1)
                        if n:
                            pe.wait_ge(eT_ready, 2 * n + side - 1)
                        for k in range(4):
                            last = nc.tensor.transpose(ps[5 + side][:, k * P:(k + 1) * P],
                                                       e_sb[:, side, k * P:(k + 1) * P], ident[:, :])
                    last.then_inc(eT_tr, 1)
                elif kind == "values":
                    c, pair, t = pair_of(n)
                    if n % 4 == 0:
                        pe.wait_ge(v_ready, GROUPS * (c + 1))
                    if n:
                        pe.wait_ge(o_ready, n)
                    for side in range(2):
                        pe.wait_ge(eT_ready, 2 * n + side + 1)
                        col = (2 * pair + side) * HD
                        for k, (g, kt) in enumerate(((0, 0), (0, 1), (1, t), (2, t))):
                            last = nc.tensor.matmul(ps[7][:, side * HD:(side + 1) * HD], eT[:, side, k * P:(k + 1) * P],
                                                    v_sb[:, c % 2, g, kt, col:col + HD], start=k == 0, stop=k == 3)
                    last.then_inc(pv_ready, 1)
                elif kind == "turn out":
                    if n == 0:
                        pe.wait_ge(qkT_ready, N_QKV * 2 // 3)
                    pe.wait_ge(o_ready, 4 * (n + 1))
                    turn_output(n)
                elif kind == "piece":
                    project(n)
                elif kind == "turn x":
                    pe.wait_ge(wo_added, 4 * QUARTERS - 2 + 2 * n)
                    turn(x, 2 * n)
                    turn(x, 2 * n + 1)

            for s, (kind, b) in enumerate(DENSE_SEQ):
                u = U_DENSE + s
                if (kind == "gate" and b) or s == len(DENSE_SEQ) - 1:
                    d = b - 1 if kind == "gate" else b
                    pe.wait_ge(dh_ready, d + 1)
                    if d:
                        pe.wait_ge(dlo_ready, d)
                    for k in range(2):
                        for t in range(TT):
                            c = k * SEQ + t * P
                            last = nc.tensor.transpose(ps[6][:, c:c + P], dh[:, t, k * P:(k + 1) * P], ident[:, :])
                    last.then_inc(dtr_ready, 1)
                pe.wait_ge(lo_ready, u + 1)
                if kind == "gate":
                    if b:
                        pe.wait_ge(dsilu_ready, b)
                    full_unit(u, ps[4], None if b else KD + QUARTERS)
                elif kind == "up":
                    if b:
                        pe.wait_ge(dh_ready, b)
                    full_unit(u, ps[5])
                else:
                    pe.wait_ge(dlo_ready, b + 1)
                    for k in range(2):
                        for t in range(TT):
                            for n in range(2):
                                last = product(ps[2 * t + n][:, :], dhT_hi[:, k, t * P:(t + 1) * P],
                                               dhT_lo[:, k, t * P:(t + 1) * P], halves(u, k * D + n * 512, 512),
                                               b == 0 and k == 0, b == N_FB - 1 and k == 1)
                    last.then_inc(unit_used, 1)

            def window(g):
                for k in (2 * g, 2 * g + 1):
                    for t in range(TT):
                        c = slice(k * P, (k + 1) * P)
                        bank = ps[4 + g][:, k % 2 * SEQ:(k % 2 + 1) * SEQ]
                        moving = poolmat[:, g, t, :]
                        nc.tensor.matmul(bank, hn_hi[:, t, c], moving, start=t == 0, stop=False)
                        last = nc.tensor.matmul(bank, (y_hi, y_lo)[t][:, c], moving, start=False, stop=t == TT - 1)
                last.then_inc(tr_ready, 1)

            def pool_map(g):
                pe.wait_ge(a_lo_ready, 2 * KD + QUARTERS + 2 * g + 2)
                for t in range(TT):
                    for k in (2 * g, 2 * g + 1):
                        hi, lo = act_of(k, t)
                        last = product(ps[2 * t + g // 2][:, g % 2 * 256:(g % 2 + 1) * 256], hi, lo,
                                       halves(U_POOL, k * 256, 256), k == 2 * g, k == 2 * g + 1)
                return last

            pe.wait_ge(poolmat_ready, 1)
            pe.wait_ge(pool_hi_ready, TT)
            pe.wait_ge(pool_lo_ready, TT)
            window(0)
            window(1)
            window(2)
            pe.wait_ge(lo_ready, U_POOL + 1)
            pool_map(0)
            window(3)
            pool_map(1).then_inc(pooled, 1)
            pool_map(2)
            pool_map(3).then_inc(unit_used, 1)

            def logits(tiles):
                for k in tiles:
                    if k % 2 == 0:
                        pe.wait_ge((hT_ready, hT1_ready)[k // 2 % 2], k // 4 + 1)
                    for t in range(TT):
                        last = nc.tensor.matmul(ps[2 * t][:, 0:E], hT[:, k, t * P:(t + 1) * P], router_g[:, k, :],
                                                start=k == 0, stop=k == KD - 1)
                return last

            pe.wait_ge(router_ready, 1)
            pe.wait_ge(pool_added, 2)
            turn(x, 0)
            turn(x, 1)
            logits(range(2))
            pe.wait_ge(pool_added, 4)
            turn(x, 2)
            turn(x, 3)
            logits(range(2, KD)).then_inc(logits_ready, 1)
            pe.wait_ge(sel_ready, 1)
            pe.wait_ge(consts_landed, CONSTS)
            for t in range(TT):
                for k in range(TT):
                    last = nc.tensor.matmul(ps[1][:, t * E:(t + 1) * E], before[:, k, t * P:(t + 1) * P], route[:, k, 4, :],
                                            start=k == 0, stop=k == TT - 1)
            last.then_inc(prefix_ready, 1)
            def gather(g):
                for n in range(2):
                    for src, bank in ((a_hi, ps[(3, 5)[n]]), (a_lo, ps[(2, 4)[n]])):
                        for q in range(4):
                            for t in range(TT):
                                c = t * D + (4 * n + q) * P
                                last = nc.tensor.matmul(bank[:, q * P:(q + 1) * P], src[:, c:c + P],
                                                        pick[:, t, :], start=t == 0, stop=t == TT - 1)
                        last.then_inc(gather_ready, 1)

            def turn_hidden(i, b):
                pe.wait_ge(h_ready, START + i * N_EB + b + 1)
                pe.wait_ge(hT_lo_ready, START + i * N_EB + b)
                if b == 0:
                    pe.wait_ge(x_added, START + 4 * i)
                for q in range(4):
                    last = nc.tensor.transpose(ps[6][:, q * P:(q + 1) * P], h[:, q * P:(q + 1) * P], ident[:, :])
                last.then_inc(htr_ready, 1)

            def expert(i, last_one):
                at = U_MOE + i * UE
                for j, (kind, b, half) in enumerate(MOE_SEQ):
                    u = U_MOE + j
                    if kind == "gate" and b == 0:
                        pe.wait_ge(xg_hi_ready, 2 * i + half + 1)
                        pe.wait_ge(xg_lo_ready, 2 * i + half + 1)
                    if kind == "gate" and half == 0:
                        if b == 1:
                            pe.wait_ge(x_added, START + 4 * i)
                        elif b:
                            pe.wait_ge(h_ready, START + i * N_EB + b - 1)
                    if kind == "down" and half == 0:
                        pe.wait_ge(hT_lo_ready, START + i * N_EB + b + 1)
                        if b == 0:
                            pe.wait_ge(y_lo_ready, START + 2 * i)
                    pe.wait_ge(lo_ready, at + j + 1)
                    if kind == "down":
                        h_hi, h_lo = hidden_T(b)
                        for k in range(2):
                            for n in range(2):
                                first = b == 0 and half == 0 and k == 0
                                final = b == N_EB - 1 and half == 1 and k == 1
                                last = product(ps[n][:, :], h_hi[:, 2 * half + k, :], h_lo[:, 2 * half + k, :],
                                               halves(u, k * D + n * 512, 512), first, final)
                    else:
                        bank = ps[(2 if kind == "gate" else 4) + b % 2]
                        for k in range(4):
                            q = 4 * half + k
                            last = product(bank[:, :], xg_hi[:, q, :], xg_lo[:, q, :], halves(u, k * 512, 512),
                                           q == 0, q == KD - 1)
                    last.then_inc(unit_used, 1)
                    if kind == "gate" and half == 0 and b:
                        turn_hidden(i, b - 1)
                    if (kind, b, half) == ("up", 1, 0):
                        pe.wait_ge(x_added, START + 4 * i)
                        for t in range(TT):
                            last = nc.tensor.transpose(ps[7][:, t * P:(t + 1) * P], pick[:, t, :].bitcast(F32), ident[:, :])
                        last.then_inc(place_tr, 1)
                    if (kind, b, half) == ("down", N_EB - 2, 0):
                        turn_hidden(i, N_EB - 1)
                if not last_one:
                    pe.wait_ge(pick_ready, TT * (i + 2))
                    gather(i + 1)
                pe.wait_ge(place_ready, i + 1)
                for q, (n, t, bank) in enumerate(SCATTER):
                    if t == 0:
                        pe.wait_ge(y_lo_ready, START + 2 * i + n + 1)
                    if q == 2 and not last_one:
                        pe.wait_ge(xg_hi_ready, 2 * i + 4)
                    cols = slice(n * 512, (n + 1) * 512)
                    nc.tensor.matmul(ps[bank][:, :], place[:, t * P:(t + 1) * P], y_hi[:, cols], start=True, stop=False)
                    nc.tensor.matmul(ps[bank][:, :], place[:, t * P:(t + 1) * P], y_lo[:, cols], start=False, stop=True)\
                        .then_inc(scatter_ready, 1)

            def round_of_experts(first):
                pe.wait_ge(pick_ready, TT * (first + 1))
                if first:
                    pe.wait_ge(x_added, START + 4 * first)
                pe.wait_ge(hnsplit_hi, TT)
                pe.wait_ge(hnsplit_lo, TT)
                gather(first)
                if not first:
                    pe.wait_ge(over_ready, 1)
                    nc.tensor.matmul(ps[7][:, 0:1], ones[:, :], over[:, 0:1], start=True, stop=True)\
                        .then_inc(overs_summed, 1)
                with pe.Fori(0, E - 1) as e:
                    expert(e + first, False)
                expert(first + E - 1, True)

            pe.sem_inc(htr_ready, START)
            round_of_experts(0)
            pe.wait_ge(routed, 1)
            more = pe.value_load(over_i[0:1, 0:1], min_val=0, max_val=1)
            with pe.If(more != 0):
                round_of_experts(E)
                pe.nop()
            with pe.Else():
                pe.nop()


def shape_constants():
    import numpy as np

    order = np.arange(SEQ).reshape(16, 4, 4).transpose(2, 1, 0).reshape(-1)
    dist = order[:, None] - order[None, :]
    near = (dist >= 0) & (dist <= 128)
    by4 = (dist >= 0) & (dist % 4 == 0)
    by16 = (dist >= 0) & (dist % 16 == 0)
    mask = np.empty((TT, P, 4 * P), np.float32)
    for t in range(TT):
        rows = slice(t * P, (t + 1) * P)
        seen = np.concatenate([near[rows], by4[rows, rows], by16[rows, rows]], axis=1)
        mask[t] = np.where(seen, 0.0, MASKED)
    freq = (10000.0 ** (-np.arange(0, HD, 2, dtype=np.float32) / np.float32(HD))).astype(np.float32)
    angle = order[:, None].astype(np.float32) * freq[None, :]
    cos = np.concatenate([np.cos(angle)] * 2, axis=1).astype(np.float32)
    sin = np.concatenate([-np.sin(angle), np.sin(angle)], axis=1).astype(np.float32)
    pool = np.zeros((PG, SEQ, SEQ), np.float32)
    inv_count = np.zeros((SEQ, PG), np.float32)
    for g, size in enumerate(POOL_SIZES):
        count = np.minimum(order + 1, size).astype(np.float32)
        inside = (dist >= 0) & (dist < size)
        pool[g] = (inside - count[:, None] * np.eye(SEQ)).T
        inv_count[:, g] = 1 / count
    ident = np.eye(P, dtype=np.float32)
    iota = np.tile(np.arange(SEQ, dtype=np.float32), (P, 1))
    before = np.triu(np.ones((SEQ, SEQ), np.float32), 1)
    return order, dict(mask_in=mask, cos_in=cos, sin_in=sin, ident_in=ident, iota_in=iota,
                       before_in=before, poolmat_in=pool, inv_count_in=inv_count)


INPUTS = ("x", "mix_norm", "ffn_norm", "attn_w_qkv", "attn_w_o", "pool_w", "pool_scale", "dense_w_gate",
          "dense_w_up", "dense_w_down", "moe_router", "moe_w_gate", "moe_w_up", "moe_w_down", "final_norm")


def kernel(**inputs):
    import numpy as np
    import concourse.bacc as bacc
    from concourse import mybir as mb
    from concourse.bass_utils import run_bass_kernel_spmd

    order, constants = shape_constants()
    arrays = {name: np.ascontiguousarray(inputs[name]) for name in INPUTS}
    arrays["x"] = np.ascontiguousarray(arrays["x"][0][order])
    arrays.update(constants)
    columns = np.stack([arrays["mix_norm"][0], arrays["ffn_norm"][0], arrays["mix_norm"][1], arrays["ffn_norm"][1]])
    arrays["gain_col"] = np.ascontiguousarray(columns.reshape(4 * KD, P).T)
    del arrays["mix_norm"]
    nc = bacc.Bacc("TRN2", target_bir_lowering=False, num_devices=1)
    args = [nc.dram_tensor(f"in_{name}", a.shape, mb.dt.from_np(a.dtype), kind="ExternalInput").ap()
            for name, a in arrays.items()]
    args.append(nc.dram_tensor("out_0", (SEQ, D), F32, kind="ExternalOutput").ap())
    program(nc, *args)
    r = run_bass_kernel_spmd(nc, [{f"in_{name}": a for name, a in arrays.items()}], core_ids=[0])
    y = np.empty((1, SEQ, D), np.float32)
    y[0, order] = r.results[0]["out_0"]
    return y
```

```python
from contextlib import ExitStack

import concourse.bass as bass
from concourse import mybir

ALU = mybir.AluOpType
ACT = mybir.ActivationFunctionType
AX = mybir.AxisListType
F32 = mybir.dt.float32
F32R = mybir.dt.float32r
I32 = mybir.dt.int32

P = 128
SEQ = 256
TT = SEQ // P
D = 1024
KD = D // P
GROUPS = 3
HEADS = 16
HD = 64
QW = 256
QUARTERS = D // QW
QH = QW // HD
D_FF = 2816
FB = 256
N_FB = D_FF // FB
E = 8
D_FFE = 3584
EB = 512
N_EB = D_FFE // EB
POOL_SIZES = (2, 4, 8, 16)
PG = len(POOL_SIZES)
EPS = 1e-6
MASKED = -1e30
SCALE = HD ** -0.5

UNIT = 2048
RAW = 4
RING = 11
SPLIT = 3
N_QKV = QUARTERS * GROUPS * 3
U_WO = N_QKV
U_DENSE = U_WO + QUARTERS
U_POOL = U_DENSE + 3 * N_FB
U_MOE = U_POOL + 1
UE = 6 * N_EB
N_STEP = HEADS * TT // 2

DENSE_SEQ = []
for _b in range(N_FB):
    DENSE_SEQ += [("gate", _b), ("up", _b)]
    if _b:
        DENSE_SEQ.append(("down", _b - 1))
DENSE_SEQ.append(("down", N_FB - 1))

MOE_SEQ = []
for _b in range(N_EB):
    MOE_SEQ += [("gate", _b, 0), ("gate", _b, 1), ("up", _b, 0), ("up", _b, 1)]
    if _b:
        MOE_SEQ += [("down", _b - 1, 0), ("down", _b - 1, 1)]
MOE_SEQ += [("down", N_EB - 1, 0), ("down", N_EB - 1, 1)]

EXPERT_SLOT = [_j % RING for _j in range(2 * RING)]
EXPERT_SLOT += [_j % (RING - 1) for _j in range(UE - 2 * RING)]


def ring_uses(j):
    return EXPERT_SLOT[:j].count(EXPERT_SLOT[j]), EXPERT_SLOT.count(EXPERT_SLOT[j])


def slot_before(j):
    n = j - 1
    while EXPERT_SLOT[n % UE] != EXPERT_SLOT[j]:
        n -= 1
    return n


def is_v(u):
    return u % 3 == 2


def qk_index(u):
    return 2 * (u // 3) + u % 3


def pair_of(m):
    return m // 4, m % 4 // 2, m % 2


PIECES = tuple((n, t) for n in range(2) for t in range(TT))

ORDER = []
for _u in range(N_QKV):
    ORDER.append(("unit", _u))
    _c, _i = divmod(_u, 3 * GROUPS)
    if _c:
        _m = 4 * (_c - 1) + _i // 2
        if _i % 2:
            ORDER.append(("turn", _m))
        else:
            if _i:
                ORDER.append(("values", _m - 1))
            if _i < 8:
                ORDER.append(("scores", _m))
ORDER += [("turn out", 0), ("scores", 12), ("piece", 0), ("piece", 1), ("turn out", 1), ("piece", 2),
          ("split", U_WO + 2), ("turn", 12), ("scores", 13), ("piece", 3), ("turn out", 2),
          ("values", 12), ("piece", 4), ("split", U_WO + 3), ("turn", 13), ("scores", 14), ("piece", 5),
          ("values", 13), ("piece", 6), ("turn", 14), ("scores", 15), ("piece", 7), ("values", 14), ("piece", 8),
          ("turn", 15), ("piece", 9), ("values", 15), ("piece", 10), ("turn out", 3), ("piece", 11),
          ("piece", 12), ("piece", 13), ("split", U_WO + 4), ("piece", 14), ("turn x", 0), ("piece", 15),
          ("turn x", 1), ("split", U_WO + 5), ("split", U_WO + 6)]

START = 1
CONSTS = 16 * 5

SCATTER = ((0, 0, 7), (0, 1, 6), (1, 0, 3), (1, 1, 5))


def program(nc, x_in, ffn_norm, w_qkv, w_o, pool_w, pool_scale, w_gate, w_up, w_down,
            router, e_gate, e_up, e_down, final_norm, mask_in, cos_in, sin_in, ident_in, iota_in,
            before_in, poolmat_in, inv_count_in,
            gain_col_in, out):
    ctx = ExitStack()
    with ctx:
        def sb(name, shape, dt=F32, scope=ctx):
            return scope.enter_context(nc.sbuf_tensor(name, shape, dt))

        def sem(name):
            return ctx.enter_context(nc.semaphore(name))

        raw = sb("raw", [P, RAW, UNIT])
        w_hi = sb("w_hi", [P, SPLIT, UNIT], F32R)
        w_lo = sb("w_lo", [P, SPLIT, UNIT], F32R)
        a_hi = sb("a_hi", [P, KD * SEQ], F32R)
        a_lo = sb("a_lo", [P, KD * SEQ], F32R)
        x = sb("x", [P, TT, D])
        twin = ExitStack()
        hn = sb("hn", [P, TT, D], F32, twin)
        twin.close()
        hn_hi = sb("hn_hi", [P, TT, D], F32R)
        rows = sb("rows", [P, 3, D])
        gain_col = sb("gain_col", [P, 4, KD])
        ident = sb("ident", [P, P])
        iota = sb("iota", [P, SEQ])
        before = sb("before", [P, TT, SEQ])
        ones = sb("ones", [P, P])
        stat = sb("stat", [P, 5, 8])
        rstat = sb("rstat", [P, 8])
        spare = sb("spare", [P, 4])
        route = sb("route", [P, TT, 8, E])
        posm = sb("posm", [P, TT, E])
        gate_w = sb("gate_w", [P, TT, E])
        rank3 = sb("rank3", [P, 2, TT, E, E])
        inv_count = sb("inv_count", [P, TT, PG])
        tie = sb("tie", [P, E, E])
        over = sb("over", [P, E + 1])
        over_i = sb("over_i", [P, 1], I32)

        attn = ExitStack()
        qkT = sb("qkT", [P, 2, 2, GROUPS, 2, SEQ], F32, attn)
        v_sb = sb("v_sb", [P, 2, GROUPS, TT, QW], F32, attn)
        roped = sb("roped", [P, 2, 2 * SEQ], F32, attn)
        rot = sb("rot", [P, 2, 2 * SEQ], F32, attn)
        s_sb = sb("s_sb", [P, 2, 4 * P], F32, attn)
        e_sb = sb("e_sb", [P, 2, 4 * P], F32, attn)
        eT = sb("eT", [P, 2, 4 * P], F32, attn)
        mask = sb("mask", [P, TT, 4 * P], F32, attn)
        cos = sb("cos", [P, SEQ], F32, attn)
        sin = sb("sin", [P, SEQ], F32, attn)
        diag = sb("diag", [P, TT, P], F32, attn)
        softs = sb("softs", [P, 2, 4, 2], F32, attn)
        attn.close()

        raw_more = sb("raw_more", [P, 3, UNIT])
        early = ExitStack()
        dh = sb("dh", [P, TT, FB], F32, early)
        dsg = sb("dsg", [P, TT, FB], F32, early)
        dhT_hi = sb("dhT_hi", [P, 2, SEQ], F32R, early)
        dhT_lo = sb("dhT_lo", [P, 2, SEQ], F32R, early)
        twin = ExitStack()
        poolmat_in_f32 = sb("poolmat_in_f32", [P, PG, TT, SEQ], F32, twin)
        twin.close()
        poolmat = sb("poolmat", [P, PG, TT, SEQ], F32R, early)
        hT = sb("hT", [P, KD, SEQ], F32, early)
        early.close()
        raw_late = sb("raw_late", [P, 3, UNIT])
        y_hi = sb("y_hi", [P, D], F32R)
        y_lo = sb("y_lo", [P, D], F32R)
        router_sb = sb("router_sb", [P, KD, E])
        router_g = sb("router_g", [P, KD, E])
        xg_hi = sb("xg_hi", [P, KD, P], F32R)
        xg_lo = sb("xg_lo", [P, KD, P], F32R)
        sg = sb("sg", [P, EB])
        h = sb("h", [P, EB])
        hT_hi = sb("hT_hi", [P, 4, P], F32R)
        hT_lo = sb("hT_lo", [P, 4, P], F32R)
        pick = sb("pick", [P, TT, P], F32R)
        place = sb("place", [P, SEQ], F32R)


        def hidden_T(b):
            if b < N_EB - 1:
                return hT_hi, hT_lo
            return [half[:, EB:2 * EB].rearrange("p (k s) -> p k s", k=4) for half in (y_hi, y_lo)]

        def dense_hidden_T(b):
            if b < N_FB - 1:
                return dhT_hi, dhT_lo
            return [half[:, 0:2 * SEQ].rearrange("p (k t) -> p k t", k=2) for half in (y_hi, y_lo)]

        ps = [ctx.enter_context(nc.psum_tensor(f"bank{n}", [P, 512], F32)) for n in range(8)]

        x_landed, ident_landed, tables_landed = sem("x_landed"), sem("ident_landed"), sem("tables_landed")
        gains_landed = sem("gains_landed")
        consts_landed, late_landed = sem("consts_landed"), sem("late_landed")
        raw_landed = [sem(f"raw_landed{n}") for n in range(RAW)]
        ring_landed = [sem(f"ring_landed{n}") for n in range(RING)]
        first_hi_ready, first_lo_ready, y_first_ready = sem("first_hi_ready"), sem("first_lo_ready"), sem("y_first_ready")
        hi_ready, lo_ready, unit_used = sem("hi_ready"), sem("lo_ready"), sem("unit_used")
        ss_ready, var_ready, std_ready = sem("ss_ready"), sem("var_ready"), sem("std_ready")
        ss1_ready, hT1_ready = sem("ss1_ready"), sem("hT1_ready")
        rstd_ready, hn_ready = sem("rstd_ready"), sem("hn_ready")
        tr_ready, a_hi_ready, a_lo_ready = sem("tr_ready"), sem("a_hi_ready"), sem("a_lo_ready")
        rope_read, rope_ready = sem("rope_read"), sem("rope_ready")
        v_ready = sem("v_ready")
        diag_ready, spread_ready, turns_ready = sem("diag_ready"), sem("spread_ready"), sem("turns_ready")
        scores_ready, masked_ready = sem("scores_ready"), sem("masked_ready")
        bias_ready, exp_ready = sem("bias_ready"), sem("exp_ready")
        eT_tr, eT_ready, pv_ready = sem("eT_tr"), sem("eT_ready"), sem("pv_ready")
        rinv_ready, o_ready = sem("rinv_ready"), sem("o_ready")
        o_turned, piece_ready, wo_added = sem("o_turned"), sem("piece_ready"), sem("wo_added")
        router_ready = sem("router_ready")
        dsilu_ready, dh_ready, dtr_ready = sem("dsilu_ready"), sem("dh_ready"), sem("dtr_ready")
        down_ready = sem("down_ready")
        dhi_ready, dlo_ready, ffn_added = sem("dhi_ready"), sem("dlo_ready"), sem("ffn_added")
        pool_hi_ready, pool_lo_ready, poolmat_ready = sem("pool_hi_ready"), sem("pool_lo_ready"), sem("poolmat_ready")
        pooled, pool_scaled, pool_added = sem("pooled"), sem("pool_scaled"), sem("pool_added")
        hnsplit_hi, hnsplit_lo = sem("hnsplit_hi"), sem("hnsplit_lo")
        hT_ready, logits_ready, route_step = sem("hT_ready"), sem("logits_ready"), sem("route_step")
        shifted_ready, weights_exp = sem("shifted_ready"), sem("weights_exp")
        sel_ready, prefix_ready, over_ready = sem("sel_ready"), sem("prefix_ready"), sem("over_ready")
        overs_summed, routed, tie_ready = sem("overs_summed"), sem("routed"), sem("tie_ready")
        pick_ready, gather_ready = sem("pick_ready"), sem("gather_ready")
        xg_hi_ready, xg_lo_ready = sem("xg_hi_ready"), sem("xg_lo_ready")
        silu_ready, h_ready, htr_ready = sem("silu_ready"), sem("h_ready"), sem("htr_ready")
        hT_hi_ready, hT_lo_ready = sem("hT_hi_ready"), sem("hT_lo_ready")
        place_tr, place_ready = sem("place_tr"), sem("place_ready")
        y_hi_ready, y_lo_ready = sem("y_hi_ready"), sem("y_lo_ready")
        scatter_ready, x_added, out_stored = sem("scatter_ready"), sem("x_added"), sem("out_stored")

        block = ctx.enter_context(nc.Block())

        def unit_source(u):
            if u < U_WO:
                c, g, part = u // 9, u % 9 // 3, u % 3
                n = (g * 3 + part) * D + c * QW
                return w_qkv[0, :, n:n + QW].rearrange("(k p) n -> p k n", p=P)
            if u < U_DENSE:
                n = (u - U_WO) * QW
                return w_o[0, n:n + QW, :].rearrange("(k p) n -> p k n", p=P)
            if u < U_POOL:
                kind, b = DENSE_SEQ[u - U_DENSE]
                if kind == "down":
                    return w_down[0, b * FB:(b + 1) * FB, :].rearrange("(k p) n -> p k n", p=P)
                w = w_gate if kind == "gate" else w_up
                return w[0, :, b * FB:(b + 1) * FB].rearrange("(k p) n -> p k n", p=P)
            return pool_w[0].rearrange("g (k p) n -> p (g k) n", p=P)

        def expert_source(j, e):
            kind, b, half = MOE_SEQ[j]
            if kind == "down":
                r = b * EB + half * 256
                return e_down[0, bass.ds(e, 1), r:r + 256, :].rearrange("a (k p) n -> p (a k) n", p=P)
            w = e_gate if kind == "gate" else e_up
            return w[0, bass.ds(e, 1), half * 512:(half + 1) * 512, b * EB:(b + 1) * EB]\
                .rearrange("a (k p) n -> p (a k) n", p=P)

        ring = [raw_more[:, n, :] for n in range(3)]
        ring += [raw[:, (U_MOE + n) % RAW, :] for n in range(RAW)]
        ring += [raw_late[:, n, :] for n in range(3)]
        ring.append(hn[:, :, :].rearrange("p t d -> p (t d)"))

        def home(u, i=0):
            if u < U_MOE:
                return raw[:, u % RAW, :], raw_landed[u % RAW], 16 * (u // RAW + 1)
            e, j = divmod(u - U_MOE, UE)
            before, uses = ring_uses(j)
            slot = EXPERT_SLOT[j]
            return ring[slot], ring_landed[slot], 16 * (before + 1 + uses * e) + 16 * uses * i

        def split_hi(act, u, i=0):
            where, landed, value = home(u, i)
            act.wait_ge(landed, value)
            if u >= SPLIT:
                act.wait_ge(unit_used, u + 1 - SPLIT + UE * i)
            nc.scalar.activation(w_hi[:, u % SPLIT, :], where, ACT.Copy).then_inc(hi_ready, 1)

        def split_lo(dve, u, i=0):
            dve.wait_ge(hi_ready, u + 1 + UE * i)
            nc.vector.tensor_tensor(w_lo[:, u % SPLIT, :], home(u, i)[0],
                                    w_hi[:, u % SPLIT, :].bitcast(F32), ALU.subtract).then_inc(lo_ready, 1)

        def split_last_hi(act, u, i):
            where, landed, value = home(u, i)
            act.wait_ge(landed, value)
            act.wait_ge(unit_used, u + 1 - SPLIT + UE * i)
            for half, ready in ((0, first_hi_ready), (1, hi_ready)):
                c = slice(half * UNIT // 2, (half + 1) * UNIT // 2)
                nc.scalar.activation(w_hi[:, u % SPLIT, c], where[:, c], ACT.Copy).then_inc(ready, 1)

        def split_last_lo(dve, u, i, round_):
            where = home(u, i)[0]
            for half, ready in ((0, first_lo_ready), (1, lo_ready)):
                if half == 0:
                    dve.wait_ge(first_hi_ready, round_)
                else:
                    dve.wait_ge(hi_ready, u + 1 + UE * i)
                c = slice(half * UNIT // 2, (half + 1) * UNIT // 2)
                nc.vector.tensor_tensor(w_lo[:, u % SPLIT, c], where[:, c], w_hi[:, u % SPLIT, c].bitcast(F32),
                                        ALU.subtract).then_inc(ready, 1)

        def rstd(m, t):
            return stat[:, m, 6 + t:7 + t]

        def halves(u, at, n):
            return w_hi[:, u % SPLIT, at:at + n], w_lo[:, u % SPLIT, at:at + n]

        def product(bank, hi, lo, w, start, stop):
            nc.tensor.matmul(bank, hi, w[0], start=start, stop=False)
            nc.tensor.matmul(bank, hi, w[1], start=False, stop=False)
            return nc.tensor.matmul(bank, lo, w[0], start=False, stop=stop)

        def act_of(k, t):
            c = slice(k * SEQ + t * P, k * SEQ + (t + 1) * P)
            return a_hi[:, c], a_lo[:, c]

        @block.sync
        def _(sp):
            def load(src, home):
                where, landed, _value = home
                sp.dma_start(where.rearrange("p (k n) -> p k n", k=src.shape[1]), src).then_inc(landed, 16)

            sp.dma_start(ident[:, :], ident_in).then_inc(ident_landed, 16)
            sp.dma_start(x[:, :, :], x_in.rearrange("(t p) d -> p t d", p=P)).then_inc(x_landed, 16)
            for u in range(U_MOE):
                if u >= RAW:
                    sp.wait_ge(lo_ready, u - RAW + 1)
                load(unit_source(u), home(u))

            sp.wait_ge(o_ready, N_STEP)
            late = {7: (unit_used, U_POOL),
                    8: (tr_ready, 12),
                    9: (logits_ready, 1),
                    10: (hnsplit_lo, TT)}
            for j in range(UE):
                if j in late:
                    sp.wait_ge(*late[j])
                elif j >= RING:
                    sp.wait_ge(lo_ready, U_MOE + slot_before(j) + 1)
                elif j >= 3:
                    sp.wait_ge(lo_ready, U_MOE - RAW + j - 3 + 1)
                load(expert_source(j, 0), home(U_MOE + j))

            def expert(i, e):
                for j in range(UE):
                    sp.wait_ge(lo_ready, U_MOE + slot_before(j) + 1 + i * UE)
                    load(expert_source(j, e), home(U_MOE + j, i))

            with sp.Fori(1, E) as e:
                expert(e, e)
            sp.wait_ge(routed, 1)
            more = sp.value_load(over_i[0:1, 0:1], min_val=0, max_val=1)
            with sp.If(more != 0):
                with sp.Fori(0, E) as e:
                    expert(e + E, e)
            with sp.Else():
                sp.nop()
            for q in range(2 * TT):
                t, n = q // 2, q % 2
                cols = slice(n * 512, (n + 1) * 512)
                sp.wait_ge(hn_ready, TT + q + 1)
                sp.dma_start(out[t * P:(t + 1) * P, cols], hn[:, t, cols]).then_inc(out_stored, 16)
            sp.wait_ge(out_stored, 16 * 2 * TT)

        @block.gpsimd
        def _(pool):
            nc.gpsimd.memset(spare[:, 0:1], 1.0).then_inc(tie_ready, 1)
            nc.gpsimd.memset(ones[:, :], 1.0).then_inc(tie_ready, 1)
            for e in range(E):
                if e:
                    nc.gpsimd.memset(tie[:, e, 0:e], 1.0).then_inc(tie_ready, 1)
                nc.gpsimd.memset(tie[:, e, e:E], 0.0).then_inc(tie_ready, 1)
            for n in range(N_QKV * 2 // 3):
                pool.wait_ge(rope_read, n + 1)
                c, g, part = n // (2 * GROUPS), n // 2 % GROUPS, n % 2
                if c >= 2:
                    pool.wait_ge(scores_ready, 4 * (c - 1))
                nc.gpsimd.tensor_tensor(qkT[:, c % 2, part, g].rearrange("p a t -> p (a t)"), roped[:, n % 2],
                                        rot[:, n % 2], ALU.add).then_inc(rope_ready, 1)

            pool.wait_ge(o_ready, N_STEP)
            pool.dma_start(poolmat_in_f32[:, :, :, :].rearrange("p g t n -> p (g t) n"),
                           poolmat_in.rearrange("g (t p) n -> p (g t) n", p=P)).then_inc(late_landed, 16)
            pool.dma_start(inv_count[:, :, :], inv_count_in.rearrange("(t p) g -> p t g", p=P)).then_inc(late_landed, 16)
            pool.dma_start(router_sb[:, :, :], router[0].rearrange("(k p) e -> p k e", p=P)).then_inc(late_landed, 16)

            for t in range(TT):
                pool.wait_ge(hnsplit_hi, t + 1)
                nc.gpsimd.tensor_tensor(a_lo[:, t * D:(t + 1) * D], hn[:, t, :], a_hi[:, t * D:(t + 1) * D].bitcast(F32),
                                        ALU.subtract).then_inc(hnsplit_lo, 1)

        MEMSETS = 2 * E + 1

        @block.scalar
        def _(act):
            act.dma_start(gain_col[:, :, :], gain_col_in.rearrange("p (m k) -> p m k", m=4)).then_inc(gains_landed, 16)
            def load_table(func, n=0):
                nc.scalar.activation(spare[:, 1 + n:2 + n], spare[:, 0:1], func)

            def squares(m):
                nc.scalar.activation(hn[:, 0, :], x[:, 0, :], ACT.Square, accum_out=stat[:, m, 0:1]).then_inc(ss_ready, 1)

            def root(m):
                act.wait_ge(var_ready, m + 1)
                nc.scalar.activation(stat[:, m, 4:4 + TT], stat[:, m, 2:2 + TT], ACT.Sqrt).then_inc(std_ready, 1)

            def split_turned(m, k):
                src = ps[4 + k // 2][:, k % 2 * SEQ:(k % 2 + 1) * SEQ]
                dst = a_hi[:, k * SEQ:(k + 1) * SEQ]
                nc.scalar.activation(dst, src, ACT.Copy, scale=gain_col[:, m, k:k + 1]).then_inc(a_hi_ready, 1)

            def split_all(m, turns):
                for k in range(KD):
                    if k % 2 == 0:
                        act.wait_ge(tr_ready, turns + k // 2 + 1)
                    split_turned(m, k)

            act.wait_ge(tie_ready, 1)
            load_table(ACT.Copy)
            act.wait_ge(gains_landed, 16)
            act.wait_ge(x_landed, 16)
            split_all(0, 0)
            for dst, src in ((cos[:, :], cos_in),
                             (sin[:, :], sin_in),
                             (mask[:, :, :], mask_in.rearrange("t p d -> p t d"))):
                act.dma_start(dst, src).then_inc(tables_landed, 16)
            split_hi(act, 0)
            split_hi(act, 1)
            squares(0)
            root(0)
            for dst, src in ((iota[:, :], iota_in),
                             (before[:, :, :], before_in.rearrange("(t p) d -> p t d", p=P)),
                             (rows[:, 0, :], pool_scale[0:1, :].to_broadcast([P, D])),
                             (rows[:, 1, :], ffn_norm[1:2, :].to_broadcast([P, D])),
                             (rows[:, 2, :], final_norm.rearrange("(a n) -> a n", a=1).to_broadcast([P, D]))):
                act.dma_start(dst, src).then_inc(consts_landed, 16)

            def output_halves(c):
                act.wait_ge(o_turned, c + 1)
                nc.scalar.activation(a_hi[:, c * 512:(c + 1) * 512], ps[2][:, :], ACT.Copy).then_inc(a_hi_ready, 1)

            split_hi(act, 2)
            act.wait_ge(rstd_ready, 1)
            for kind, n in ORDER:
                if kind == "unit":
                    act.wait_ge(unit_used, n + 1)
                    if is_v(n):
                        g, c = n % 9 // 3, n // 9
                        if c >= 2:
                            act.wait_ge(pv_ready, 4 * (c - 1))
                        for t in range(TT):
                            last = nc.scalar.activation(v_sb[:, c % 2, g, t], ps[n % 2][:, t * QW:(t + 1) * QW],
                                                        ACT.Copy, scale=rstd(0, t))
                        last.then_inc(v_ready, 1)
                    if n < N_QKV - 1:
                        split_hi(act, n + 3)
                elif kind == "scores":
                    for side in range(2):
                        act.wait_ge(bias_ready, 2 * n + side + 1)
                        if n:
                            act.wait_ge(eT_tr, n)
                        if n >= 2:
                            act.wait_ge(rinv_ready, n - 1)
                        nc.scalar.activation(e_sb[:, side, :], s_sb[:, side, :], ACT.Exp, scale=SCALE,
                                             bias=softs[:, n % 2, 1, side:side + 1],
                                             accum_out=softs[:, n % 2, 2, side:side + 1]).then_inc(exp_ready, 1)
                elif kind == "turn":
                    act.wait_ge(eT_tr, n + 1)
                    if n:
                        act.wait_ge(pv_ready, n)
                    for side in range(2):
                        nc.scalar.activation(eT[:, side, :], ps[5 + side][:, :], ACT.Copy).then_inc(eT_ready, 1)
                elif kind == "turn out":
                    output_halves(n)
                elif kind == "split":
                    split_hi(act, n)
                elif kind == "turn x":
                    for j in (2 * n, 2 * n + 1):
                        act.wait_ge(tr_ready, 4 + j + 1)
                        split_turned(1, 2 * j)
                        split_turned(1, 2 * j + 1)
            act.wait_ge(wo_added, 4 * QUARTERS)
            squares(1)
            root(1)
            act.wait_ge(rstd_ready, 2)

            for s, (kind, b) in enumerate(DENSE_SEQ):
                if kind == "up":
                    act.wait_ge(unit_used, U_DENSE + s)
                    if b:
                        act.wait_ge(dh_ready, b)
                    for t in range(TT):
                        last = nc.scalar.activation(dsg[:, t, :], ps[4][:, t * FB:(t + 1) * FB], ACT.Silu,
                                                    scale=rstd(1, t))
                    last.then_inc(dsilu_ready, 1)
                if (kind == "gate" and b) or s == len(DENSE_SEQ) - 2:
                    d = b - 1 if kind == "gate" else b + 1
                    act.wait_ge(dtr_ready, d + 1)
                    nc.scalar.activation(dense_hidden_T(d)[0][:, :, :], ps[6][:, :].rearrange("p (k t) -> p k t", k=2), ACT.Copy)\
                        .then_inc(dhi_ready, 1)
                if s and U_DENSE + s + 2 < U_MOE:
                    split_hi(act, U_DENSE + s + 2)
                if s == N_FB:
                    act.wait_ge(late_landed, 48)
                    nc.scalar.activation(poolmat[:, :, :, :], poolmat_in_f32[:, :, :, :], ACT.Copy)\
                        .then_inc(poolmat_ready, 1)
            split_hi(act, U_MOE)

            load_table(ACT.Sqrt, 0)
            act.wait_ge(ffn_added, 2)
            squares(2)
            root(2)
            act.wait_ge(rstd_ready, 3)
            for n, t in PIECES:
                cols = slice(n * 512, (n + 1) * 512)
                nc.scalar.activation(hn_hi[:, t, cols], x[:, t, cols], ACT.Copy, scale=rstd(2, t))\
                    .then_inc(pool_hi_ready, 1)
            split_all(2, 8)
            split_hi(act, U_MOE + 1)

            for j in range(3):
                act.wait_ge(tr_ready, 12 + j + 1)
                nc.scalar.activation(hT[:, 2 * j:2 * j + 2, :], ps[4 + j][:, :].rearrange("p (k t) -> p k t", k=2),
                                     ACT.Copy).then_inc(hT_ready, 1)
            act.wait_ge(pool_added, 4)
            squares(3)
            root(3)
            load_table(ACT.Exp, 1)
            for t in range(TT):
                act.wait_ge(hn_ready, t + 1)
                nc.scalar.activation(a_hi[:, t * D:(t + 1) * D], hn[:, t, :], ACT.Copy).then_inc(hnsplit_hi, 1)
            act.wait_ge(shifted_ready, 1)
            nc.scalar.activation(route[:, :, 2, :], route[:, :, 1, :], ACT.Exp).then_inc(weights_exp, 1)
            split_hi(act, U_MOE + 2)

            def gather(g):
                for n in range(2):
                    act.wait_ge(gather_ready, 4 * g + 2 * n + 1)
                    nc.scalar.activation(xg_hi[:, 4 * n:4 * n + 4, :],
                                         ps[(3, 5)[n]][:, :].rearrange("p (k s) -> p k s", k=4), ACT.Copy)\
                        .then_inc(xg_hi_ready, 1)

            def expert(i, last):
                at = U_MOE + i * UE
                load_table(ACT.Silu, 1)
                for j, (kind, b, half) in enumerate(MOE_SEQ):
                    if kind == "up" and half == 0:
                        act.wait_ge(unit_used, at + j)
                        act.wait_ge(h_ready, START + i * N_EB + b)
                        nc.scalar.activation(sg[:, :], ps[2 + b % 2][:, :], ACT.Silu).then_inc(silu_ready, 1)
                    if half == 1 and (kind == "gate" and b or kind == "down" and b == N_EB - 2):
                        d = b - 1 if kind == "gate" else b + 1
                        act.wait_ge(htr_ready, START + i * N_EB + d + 1)
                        nc.scalar.activation(hidden_T(d)[0][:, :, :], ps[6][:, :].rearrange("p (k s) -> p k s", k=4), ACT.Copy)\
                            .then_inc(hT_hi_ready, 1)
                    if (kind, b, half) == ("up", 1, 1):
                        act.wait_ge(place_tr, i + 1)
                        nc.scalar.activation(place[:, :], ps[7][:, 0:SEQ], ACT.Copy).then_inc(place_ready, 1)
                    if last and j + 2 == UE - 1:
                        split_last_hi(act, U_MOE + UE - 1, i)
                    elif j and (j + 2 < UE or not last):
                        split_hi(act, U_MOE + j + 2, i)
                for n in range(2):
                    if last and n == 0:
                        act.wait_ge(y_first_ready, (i + 1) // E)
                    else:
                        act.wait_ge(unit_used, at + UE)
                    nc.scalar.activation(y_hi[:, n * 512:(n + 1) * 512], ps[n][:, :], ACT.Copy)\
                        .then_inc(y_hi_ready, 1)
                if not last:
                    gather(i + 1)
                    split_hi(act, U_MOE + UE + 2, i)

            def round_of_experts(first):
                gather(first)
                with act.Fori(0, E - 1) as e:
                    expert(e + first, False)
                expert(first + E - 1, True)
                load_table(ACT.Sqrt, 2 if first else 0)
                act.wait_ge(x_added, START + 4 * (first + E))

            round_of_experts(0)
            act.wait_ge(routed, 1)
            more = act.value_load(over_i[0:1, 0:1], min_val=0, max_val=1)
            with act.If(more != 0):
                split_hi(act, U_MOE + E * UE)
                split_hi(act, U_MOE + E * UE + 1)
                split_hi(act, U_MOE + E * UE + 2)
                round_of_experts(E)
                act.nop()
            with act.Else():
                act.nop()
            squares(4)
            root(4)

        @block.vector
        def _(dve):
            dve.wait_ge(tie_ready, MEMSETS)

            def squares(m):
                nc.vector.tensor_tensor_reduce(out=hn[:, 1, :], in0=x[:, 1, :], in1=x[:, 1, :], scale=1.0, scalar=0.0,
                                               op0=ALU.mult, op1=ALU.add, accum_out=stat[:, m, 1:2])\
                    .then_inc(ss1_ready, 1)

            def mean(m):
                dve.wait_ge(ss1_ready, m + 1)
                dve.wait_ge(ss_ready, m + 1)
                nc.vector.tensor_scalar(stat[:, m, 2:2 + TT], stat[:, m, 0:TT], 1.0 / D, EPS, ALU.mult, ALU.add)\
                    .then_inc(var_ready, 1)

            def invert(m):
                dve.wait_ge(std_ready, m + 1)
                nc.vector.reciprocal(stat[:, m, 6:6 + TT], stat[:, m, 4:4 + TT]).then_inc(rstd_ready, 1)
                dve.wait_ge(rstd_ready, m + 1)

            def normed(m, row):
                for t in range(TT):
                    nc.vector.scalar_tensor_tensor(hn[:, t, :], x[:, t, :], rstd(m, t), rows[:, row, :],
                                                   ALU.mult, ALU.mult).then_inc(hn_ready, 1)

            def split_turned(m, before_these, tiles):
                for k in tiles:
                    if k % 2 == 0:
                        dve.wait_ge(a_hi_ready, before_these + k + 2)
                    cols = slice(k * SEQ, (k + 1) * SEQ)
                    nc.vector.scalar_tensor_tensor(a_lo[:, cols], ps[4 + k // 2][:, k % 2 * SEQ:(k % 2 + 1) * SEQ],
                                                   gain_col[:, m, k:k + 1], a_hi[:, cols].bitcast(F32),
                                                   ALU.mult, ALU.subtract).then_inc(a_lo_ready, 1)

            def split_all(m, before_these):
                split_turned(m, before_these, range(KD))

            def output_halves(c):
                dve.wait_ge(a_hi_ready, KD + c + 1)
                cols = slice(c * 512, (c + 1) * 512)
                nc.vector.tensor_tensor(a_lo[:, cols], ps[2][:, :], a_hi[:, cols].bitcast(F32), ALU.subtract)\
                    .then_inc(a_lo_ready, 1)

            def add_piece(q):
                n, t = PIECES[q % 4]
                if q % 4 == 3:
                    dve.wait_ge(unit_used, U_WO + q // 4 + 1)
                else:
                    dve.wait_ge(piece_ready, 3 * (q // 4) + q % 4 + 1)
                cols = x[:, t, n * 512:(n + 1) * 512]
                nc.vector.tensor_tensor(cols, cols, ps[q % 2][:, :], ALU.add).then_inc(wo_added, 1)

            dve.wait_ge(gains_landed, 16)
            split_all(0, 0)
            split_lo(dve, 0)
            split_lo(dve, 1)
            dve.wait_ge(x_landed, 16)
            squares(0)
            mean(0)
            invert(0)
            for t in range(TT):
                nc.vector.tensor_scalar(diag[:, t, :], ident[:, :], rstd(0, t), None, ALU.mult).then_inc(diag_ready, 1)
            dve.wait_ge(tables_landed, 16 * 3)
            dve.wait_ge(spread_ready, 1)
            for table in (cos, sin):
                nc.vector.tensor_tensor(table[:, :], table[:, :], ps[3][:, 0:SEQ], ALU.mult).then_inc(turns_ready, 1)

            split_lo(dve, 2)
            for kind, n in ORDER:
                if kind == "unit":
                    if not is_v(n):
                        q = qk_index(n)
                        dve.wait_ge(unit_used, n + 1)
                        if q == 0:
                            dve.wait_ge(turns_ready, 2)
                        if q >= 2:
                            dve.wait_ge(rope_ready, q - 1)
                        bank = ps[n % 2][:, :].rearrange("p (a t) -> p a t", a=2)
                        straight = roped[:, q % 2].rearrange("p (a t) -> p a t", a=2)
                        turned = rot[:, q % 2].rearrange("p (a t) -> p a t", a=2)
                        nc.vector.tensor_tensor(straight, bank, cos[:, :].unsqueeze(1).to_broadcast([P, 2, SEQ]), ALU.mult)
                        h2 = HD // 2
                        for at in range(0, P, HD):
                            for to, of in ((at, at + h2), (at + h2, at)):
                                last = nc.vector.tensor_tensor(
                                    turned[to:to + h2], bank[of:of + h2],
                                    sin[of:of + h2, :].unsqueeze(1).to_broadcast([h2, 2, SEQ]), ALU.mult)
                        last.then_inc(rope_read, 1)
                    if n < N_QKV - 1:
                        split_lo(dve, n + 3)
                elif kind == "scores":
                    t = pair_of(n)[2]
                    dve.wait_ge(scores_ready, n + 1)
                    for side in range(2):
                        if n:
                            dve.wait_ge(exp_ready, 2 * n + side - 1)
                        if n >= 2:
                            dve.wait_ge(o_ready, n - 1)
                        nc.vector.tensor_tensor_reduce(out=s_sb[:, side, :], in0=ps[3 + side][:, :], in1=mask[:, t, :],
                                                       scale=1.0, scalar=-3e38, op0=ALU.add, op1=ALU.max,
                                                       accum_out=softs[:, n % 2, 0, side:side + 1])\
                            .then_inc(masked_ready, 1)
                        dve.wait_ge(masked_ready, 2 * n + side + 1)
                        nc.vector.tensor_scalar(softs[:, n % 2, 1, side:side + 1], softs[:, n % 2, 0, side:side + 1],
                                                -SCALE, None, ALU.mult).then_inc(bias_ready, 1)
                elif kind == "values":
                    c, pair, t = pair_of(n)
                    at = (c * QH + 2 * pair) * HD
                    dve.wait_ge(exp_ready, 2 * n + 2)
                    nc.vector.reciprocal(softs[:, n % 2, 3, :], softs[:, n % 2, 2, :]).then_inc(rinv_ready, 1)
                    dve.wait_ge(rinv_ready, n + 1)
                    dve.wait_ge(pv_ready, n + 1)
                    nc.vector.tensor_tensor(hn[:, t, at:at + 2 * HD].rearrange("p (a n) -> p a n", a=2),
                                            ps[7][:, 0:2 * HD].rearrange("p (a n) -> p a n", a=2),
                                            softs[:, n % 2, 3, :].unsqueeze(2).to_broadcast([P, 2, HD]), ALU.mult)\
                        .then_inc(o_ready, 1)
                elif kind == "turn out":
                    output_halves(n)
                elif kind == "piece":
                    add_piece(n)
                elif kind == "split":
                    split_lo(dve, n)
                elif kind == "turn x" and n:
                    split_all(1, KD + QUARTERS)
            dve.wait_ge(wo_added, 4 * QUARTERS)
            squares(1)
            mean(1)
            invert(1)

            for s, (kind, b) in enumerate(DENSE_SEQ):
                if s and DENSE_SEQ[s - 1][0] == "up":
                    d = DENSE_SEQ[s - 1][1]
                    dve.wait_ge(unit_used, U_DENSE + s)
                    dve.wait_ge(dsilu_ready, d + 1)
                    if d:
                        dve.wait_ge(dtr_ready, d)
                    for t in range(TT):
                        last = nc.vector.scalar_tensor_tensor(dh[:, t, :], ps[5][:, t * FB:(t + 1) * FB], rstd(1, t),
                                                              dsg[:, t, :], ALU.mult, ALU.mult)
                    last.then_inc(dh_ready, 1)
                    if d == 0:
                        split_lo(dve, U_DENSE + 3)
                if (kind == "gate" and b) or s == len(DENSE_SEQ) - 2:
                    d = b - 1 if kind == "gate" else b + 1
                    dve.wait_ge(dhi_ready, d + 1)
                    h_hi, h_lo = dense_hidden_T(d)
                    nc.vector.tensor_tensor(h_lo[:, :, :], ps[6][:, :].rearrange("p (k t) -> p k t", k=2),
                                            h_hi[:, :, :].bitcast(F32), ALU.subtract).then_inc(dlo_ready, 1)
                if s > 1 and U_DENSE + s + 2 < U_MOE:
                    split_lo(dve, U_DENSE + s + 2)
            split_lo(dve, U_MOE)
            for t in range(TT):
                for n in range(2):
                    if 2 * t + n < 3:
                        dve.wait_ge(down_ready, 2 * t + n + 1)
                    else:
                        dve.wait_ge(unit_used, U_POOL)
                    cols = x[:, t, n * 512:(n + 1) * 512]
                    nc.vector.tensor_tensor(cols, cols, ps[2 * t + n][:, :], ALU.add).then_inc(ffn_added, 1)
            dve.wait_ge(ffn_added, 4)
            squares(2)
            mean(2)
            invert(2)
            for q, (n, t) in enumerate(PIECES):
                dve.wait_ge(pool_hi_ready, q + 1)
                cols = slice(n * 512, (n + 1) * 512)
                nc.vector.scalar_tensor_tensor((y_hi, y_lo)[t][:, cols], x[:, t, cols], rstd(2, t),
                                               hn_hi[:, t, cols].bitcast(F32),
                                               ALU.mult, ALU.subtract).then_inc(pool_lo_ready, 1)
            dve.wait_ge(late_landed, 48)
            nc.vector.tensor_tensor(router_g[:, :, :], router_sb[:, :, :],
                                    gain_col[:, 3, :].unsqueeze(2).to_broadcast([P, KD, E]), ALU.mult)\
                .then_inc(router_ready, 1)
            split_all(2, 2 * KD + QUARTERS)

            dve.wait_ge(consts_landed, CONSTS)
            for q, (n, t) in enumerate(PIECES):
                if n == 0:
                    dve.wait_ge(pooled, 1)
                else:
                    dve.wait_ge(unit_used, U_POOL + 1)
                for g in (2 * n, 2 * n + 1):
                    c = slice(g * 256, (g + 1) * 256)
                    last = nc.vector.scalar_tensor_tensor(hn[:, t, c], ps[2 * t + n][:, g % 2 * 256:(g % 2 + 1) * 256],
                                                          inv_count[:, t, g:g + 1], rows[:, 0, c], ALU.mult, ALU.mult)
                last.then_inc(pool_scaled, 1)
                dve.wait_ge(pool_scaled, q + 1)
                cols = slice(n * 512, (n + 1) * 512)
                nc.vector.tensor_tensor(x[:, t, cols], x[:, t, cols], hn[:, t, cols], ALU.add)\
                    .then_inc(pool_added, 1)
            dve.wait_ge(tr_ready, 16)
            nc.vector.tensor_copy(hT[:, 6:8, :], ps[7][:, :].rearrange("p (k t) -> p k t", k=2)).then_inc(hT1_ready, 1)
            dve.wait_ge(pool_added, 4)
            squares(3)
            mean(3)
            invert(3)
            normed(3, 1)

            steps = [0]

            def chain(instruction):
                steps[0] += 1
                instruction.then_inc(route_step, 1)
                dve.wait_ge(route_step, steps[0])

            dve.wait_ge(logits_ready, 1)
            lg, shifted, ex, rank, sel, wt, pos, far = (route[:, :, n, :] for n in range(8))
            nc.vector.tensor_scalar(lg[:, 0], ps[0][:, 0:E], rstd(3, 0), None, ALU.mult)
            chain(nc.vector.tensor_scalar(lg[:, 1], ps[2][:, 0:E], rstd(3, 1), None, ALU.mult))
            chain(nc.vector.tensor_reduce(rstat[:, 0:TT], lg, AX.X, ALU.max))
            nc.vector.tensor_tensor(shifted, lg, rstat[:, 0:TT].unsqueeze(2).to_broadcast([P, TT, E]), ALU.subtract)\
                .then_inc(shifted_ready, 1)
            other = lg.unsqueeze(2).to_broadcast([P, TT, E, E])
            own = lg.unsqueeze(3).to_broadcast([P, TT, E, E])
            chain(nc.vector.tensor_tensor(rank3[:, 1], other, own, ALU.is_equal))
            chain(nc.vector.tensor_tensor(rank3[:, 1], rank3[:, 1], tie[:, :, :].unsqueeze(1).to_broadcast([P, TT, E, E]),
                                          ALU.mult))
            chain(nc.vector.tensor_tensor(rank3[:, 0], other, own, ALU.is_gt))
            chain(nc.vector.tensor_tensor(rank3[:, 0], rank3[:, 0], rank3[:, 1], ALU.add))
            chain(nc.vector.tensor_reduce(rank, rank3[:, 0], AX.X, ALU.add))
            nc.vector.tensor_scalar(sel, rank, 2.0, None, ALU.is_lt).then_inc(sel_ready, 1)
            dve.wait_ge(sel_ready, 1)
            dve.wait_ge(weights_exp, 1)
            chain(nc.vector.tensor_tensor(wt, ex, sel, ALU.mult))
            chain(nc.vector.tensor_reduce(rstat[:, 2:2 + TT], wt, AX.X, ALU.add))
            chain(nc.vector.reciprocal(rstat[:, 4:4 + TT], rstat[:, 2:2 + TT]))
            chain(nc.vector.tensor_tensor(gate_w[:, :, :], wt, rstat[:, 4:4 + TT].unsqueeze(2).to_broadcast([P, TT, E]),
                                          ALU.mult))
            dve.wait_ge(prefix_ready, 1)
            chain(nc.vector.scalar_tensor_tensor(pos, ps[1][:, 0:TT * E].rearrange("p (t e) -> p t e", t=TT), 1.0,
                                                 sel, ALU.add, ALU.mult))
            chain(nc.vector.tensor_scalar(posm[:, :, :], pos, -1.0, None, ALU.add))
            def pick_slots(i, first):
                shift = 0 if first == 0 else P
                for t in range(TT):
                    nc.vector.tensor_scalar(pick[:, t, :], iota[:, shift:shift + P], posm[:, t, bass.ds(i - first, 1)],
                                            None, ALU.is_equal).then_inc(pick_ready, 1)

            def gather(g):
                for n in range(2):
                    dve.wait_ge(gather_ready, 4 * g + 2 * n + 2)
                    nc.vector.tensor_copy(xg_lo[:, 4 * n:4 * n + 4, :],
                                          ps[(2, 4)[n]][:, :].rearrange("p (k s) -> p k s", k=4)).then_inc(xg_lo_ready, 1)

            def expert(i, first, last):
                at = U_MOE + i * UE
                for j, (kind, b, half) in enumerate(MOE_SEQ):
                    if j and MOE_SEQ[j - 1][0] == "up" and MOE_SEQ[j - 1][2] == 1:
                        d = MOE_SEQ[j - 1][1] + i * N_EB
                        dve.wait_ge(unit_used, at + j)
                        dve.wait_ge(silu_ready, d + 1)
                        dve.wait_ge(htr_ready, START + d)
                        nc.vector.tensor_tensor(h[:, :], sg[:, :], ps[4 + MOE_SEQ[j - 1][1] % 2][:, :], ALU.mult)\
                            .then_inc(h_ready, 1)
                    if half == 1 and (kind == "gate" and b or kind == "down" and b == N_EB - 2):
                        d = b - 1 if kind == "gate" else b + 1
                        dve.wait_ge(hT_hi_ready, i * N_EB + d + 1)
                        h_hi, h_lo = hidden_T(d)
                        nc.vector.tensor_tensor(h_lo[:, :, :], ps[6][:, :].rearrange("p (k s) -> p k s", k=4),
                                                h_hi[:, :, :].bitcast(F32), ALU.subtract).then_inc(hT_lo_ready, 1)
                    if (kind, b, half) == ("gate", 3, 0) and not last:
                        dve.wait_ge(place_tr, i + 1)
                        pick_slots(i + 1, first)
                    if last and j + 2 == UE - 1:
                        split_last_lo(dve, U_MOE + UE - 1, i, (i + 1) // E)
                    elif j and (j + 2 < UE or not last):
                        split_lo(dve, U_MOE + j + 2, i)
                for n in range(2):
                    dve.wait_ge(y_hi_ready, 2 * i + n + 1)
                    cols = slice(n * 512, (n + 1) * 512)
                    nc.vector.tensor_tensor(y_lo[:, cols], ps[n][:, :], y_hi[:, cols].bitcast(F32), ALU.subtract)\
                        .then_inc(y_lo_ready, 1)
                if not last:
                    gather(i + 1)
                for q, (n, t, bank) in enumerate(SCATTER):
                    dve.wait_ge(scatter_ready, 4 * i + q + 1)
                    cols = x[:, t, n * 512:(n + 1) * 512]
                    nc.vector.scalar_tensor_tensor(cols, ps[bank][:, :], gate_w[:, t, bass.ds(i - first, 1)], cols,
                                                   ALU.mult, ALU.add).then_inc(x_added, 1)
                if not last:
                    split_lo(dve, U_MOE + UE + 2, i)

            def round_of_experts(first):
                if first:
                    pick_slots(first, first)
                else:
                    split_lo(dve, U_MOE + 1)
                gather(first)
                if not first:
                    split_lo(dve, U_MOE + 2)
                if not first:
                    dve.wait_ge(overs_summed, 1)
                    nc.vector.tensor_scalar(over_i[:, :], ps[7][:, 0:1], 1.0, None, ALU.min).then_inc(routed, 1)
                with dve.Fori(0, E - 1) as e:
                    expert(e + first, first, False)
                expert(first + E - 1, first, True)
                dve.wait_ge(x_added, START + 4 * (first + E))

            for counter in (h_ready, hT_lo_ready, x_added, y_lo_ready):
                dve.sem_inc(counter, START)
            pick_slots(0, 0)
            chain(nc.vector.tensor_scalar(far, posm[:, :, :], float(P), None, ALU.is_ge))
            nc.vector.tensor_reduce(over[:, 0:1], far, AX.XY, ALU.add).then_inc(over_ready, 1)
            round_of_experts(0)
            more = dve.value_load(over_i[0:1, 0:1], min_val=0, max_val=1)
            with dve.If(more != 0):
                split_lo(dve, U_MOE + E * UE)
                split_lo(dve, U_MOE + E * UE + 1)
                split_lo(dve, U_MOE + E * UE + 2)
                round_of_experts(E)
                dve.nop()
            with dve.Else():
                dve.nop()
            squares(4)
            mean(4)
            invert(4)
            for t in range(TT):
                for n in range(2):
                    cols = slice(n * 512, (n + 1) * 512)
                    nc.vector.scalar_tensor_tensor(hn[:, t, cols], x[:, t, cols], rstd(4, t), rows[:, 2, cols],
                                                   ALU.mult, ALU.mult).then_inc(hn_ready, 1)

        @block.tensor
        def _(pe):
            def turn(src, j):
                for k in range(2):
                    for t in range(TT):
                        c = (2 * j + k) * P
                        last = nc.tensor.transpose(ps[4 + j][:, k * SEQ + t * P:k * SEQ + (t + 1) * P],
                                                   src[:, t, c:c + P], ident[:, :])
                last.then_inc(tr_ready, 1)

            def turn_output(c):
                if c:
                    pe.wait_ge(a_lo_ready, KD + c)
                for k in range(2):
                    for t in range(TT):
                        last = nc.tensor.transpose(ps[2][:, k * SEQ + t * P:k * SEQ + (t + 1) * P],
                                                   hn[:, t, (2 * c + k) * P:(2 * c + k + 1) * P], ident[:, :])
                last.then_inc(o_turned, 1)

            def project(q):
                c, (n, t) = q // 4, PIECES[q % 4]
                pe.wait_ge(a_lo_ready, KD + c + 1)
                pe.wait_ge(lo_ready, U_WO + c + 1)
                if q >= 2:
                    pe.wait_ge(wo_added, q - 1)
                elif q == 0:
                    pe.wait_ge(rope_read, qk_index(N_QKV - 2) + 1)
                else:
                    pe.wait_ge(v_ready, N_QKV // 3)
                for k in range(2):
                    hi, lo = act_of(2 * c + k, t)
                    last = product(ps[q % 2][:, :], hi, lo, halves(U_WO + c, k * D + n * 512, 512), k == 0, k == 1)
                last.then_inc(unit_used if q % 4 == 3 else piece_ready, 1)

            def full_unit(u, bank, before=None):
                for t in range(TT):
                    for k in range(KD):
                        if before is not None and t == 0 and k % 2 == 0:
                            pe.wait_ge(a_lo_ready, before + k + 2)
                        hi, lo = act_of(k, t)
                        last = product(bank[:, t * QW:(t + 1) * QW], hi, lo, halves(u, k * QW, QW), k == 0, k == KD - 1)
                last.then_inc(unit_used, 1)

            def full_unit_turned(u, bank, before=None):
                for pair in range(2):
                    for k in range(KD):
                        if before is not None and pair == 0 and k % 2 == 0:
                            pe.wait_ge(a_lo_ready, before + k + 2)
                        hi, lo = halves(u, k * QW + pair * P, P)
                        c = slice(k * SEQ, (k + 1) * SEQ)
                        last = product(bank[:, pair * SEQ:(pair + 1) * SEQ], hi, lo, (a_hi[:, c], a_lo[:, c]),
                                       k == 0, k == KD - 1)
                last.then_inc(unit_used, 1)

            pe.wait_ge(ident_landed, 16)
            pe.wait_ge(x_landed, 16)
            for j in range(4):
                turn(x, j)

            for kind, n in ORDER:
                if kind == "unit":
                    pe.wait_ge(lo_ready, n + 1)
                    if n >= 2 and is_v(n - 2):
                        pe.wait_ge(v_ready, (n - 2) // 3 + 1)
                    elif n >= 2:
                        pe.wait_ge(rope_read, qk_index(n - 2) + 1)
                    if is_v(n):
                        full_unit(n, ps[n % 2])
                    else:
                        full_unit_turned(n, ps[n % 2], None if n else 0)
                    if n == 0:
                        pe.wait_ge(diag_ready, TT)
                        pe.wait_ge(tie_ready, MEMSETS)
                        for t in range(TT):
                            last = nc.tensor.matmul(ps[3][:, t * P:(t + 1) * P], ones[:, :], diag[:, t, :],
                                                    start=True, stop=True)
                        last.then_inc(spread_ready, 1)
                elif kind == "scores":
                    c, pair, t = pair_of(n)
                    if n % 4 == 0:
                        pe.wait_ge(rope_ready, 2 * GROUPS * (c + 1))
                    if n:
                        pe.wait_ge(masked_ready, 2 * n)
                    for g, at, k0, kn in ((0, 0, 0, SEQ), (1, SEQ, t * P, P), (2, SEQ + P, t * P, P)):
                        for side in range(2):
                            part = slice(side * HD, (side + 1) * HD)
                            last = nc.tensor.matmul(ps[3 + side][:, at:at + kn],
                                                    qkT[part, c % 2, 0, g, pair, t * P:(t + 1) * P],
                                                    qkT[part, c % 2, 1, g, pair, k0:k0 + kn], start=True, stop=True)
                    last.then_inc(scores_ready, 1)
                elif kind == "turn":
                    for side in range(2):
                        pe.wait_ge(exp_ready, 2 * n + side + 1)
                        if n:
                            pe.wait_ge(eT_ready, 2 * n + side - 1)
                        for k in range(4):
                            last = nc.tensor.transpose(ps[5 + side][:, k * P:(k + 1) * P],
                                                       e_sb[:, side, k * P:(k + 1) * P], ident[:, :])
                    last.then_inc(eT_tr, 1)
                elif kind == "values":
                    c, pair, t = pair_of(n)
                    if n % 4 == 0:
                        pe.wait_ge(v_ready, GROUPS * (c + 1))
                    if n:
                        pe.wait_ge(o_ready, n)
                    for side in range(2):
                        pe.wait_ge(eT_ready, 2 * n + side + 1)
                        col = (2 * pair + side) * HD
                        for k, (g, kt) in enumerate(((0, 0), (0, 1), (1, t), (2, t))):
                            last = nc.tensor.matmul(ps[7][:, side * HD:(side + 1) * HD], eT[:, side, k * P:(k + 1) * P],
                                                    v_sb[:, c % 2, g, kt, col:col + HD], start=k == 0, stop=k == 3)
                    last.then_inc(pv_ready, 1)
                elif kind == "turn out":
                    pe.wait_ge(o_ready, 4 * (n + 1))
                    turn_output(n)
                elif kind == "piece":
                    project(n)
                elif kind == "turn x":
                    pe.wait_ge(wo_added, 4 * QUARTERS - 2 + 2 * n)
                    turn(x, 2 * n)
                    turn(x, 2 * n + 1)

            def turn_dense_hidden(b):
                pe.wait_ge(dh_ready, b + 1)
                if b:
                    pe.wait_ge(dlo_ready, b)
                for k in range(2):
                    for t in range(TT):
                        c = k * SEQ + t * P
                        last = nc.tensor.transpose(ps[6][:, c:c + P], dh[:, t, k * P:(k + 1) * P], ident[:, :])
                last.then_inc(dtr_ready, 1)

            def down_part(b, k, t, n):
                h_hi, h_lo = dense_hidden_T(b)
                return product(ps[2 * t + n][:, :], h_hi[:, k, t * P:(t + 1) * P], h_lo[:, k, t * P:(t + 1) * P],
                               halves(U_DENSE + s, k * D + n * 512, 512), b == 0 and k == 0, b == N_FB - 1 and k == 1)

            for s, (kind, b) in enumerate(DENSE_SEQ):
                u = U_DENSE + s
                if kind == "gate" and b:
                    turn_dense_hidden(b - 1)
                pe.wait_ge(lo_ready, u + 1)
                if kind == "gate":
                    if b:
                        pe.wait_ge(dsilu_ready, b)
                    full_unit(u, ps[4], None if b else KD + QUARTERS)
                elif kind == "up":
                    if b:
                        pe.wait_ge(dh_ready, b)
                    full_unit(u, ps[5])
                elif b < N_FB - 1:
                    pe.wait_ge(dlo_ready, b + 1)
                    for k in range(2):
                        for t in range(TT):
                            for n in range(2):
                                last = down_part(b, k, t, n)
                        if k == 0 and b == N_FB - 2:
                            turn_dense_hidden(N_FB - 1)
                    last.then_inc(unit_used, 1)
                else:
                    pe.wait_ge(dlo_ready, b + 1)
                    for t in range(TT):
                        for n in range(2):
                            down_part(b, 0, t, n)
                            last = down_part(b, 1, t, n)
                            last.then_inc(down_ready if 2 * t + n < 3 else unit_used, 1)

            def window(g):
                for k in (2 * g, 2 * g + 1):
                    for t in range(TT):
                        c = slice(k * P, (k + 1) * P)
                        bank = ps[4 + g][:, k % 2 * SEQ:(k % 2 + 1) * SEQ]
                        moving = poolmat[:, g, t, :]
                        nc.tensor.matmul(bank, hn_hi[:, t, c], moving, start=t == 0, stop=False)
                        last = nc.tensor.matmul(bank, (y_hi, y_lo)[t][:, c], moving, start=False, stop=t == TT - 1)
                last.then_inc(tr_ready, 1)

            def pool_map(g):
                pe.wait_ge(a_lo_ready, 2 * KD + QUARTERS + 2 * g + 2)
                for t in range(TT):
                    for k in (2 * g, 2 * g + 1):
                        hi, lo = act_of(k, t)
                        last = product(ps[2 * t + g // 2][:, g % 2 * 256:(g % 2 + 1) * 256], hi, lo,
                                       halves(U_POOL, k * 256, 256), k == 2 * g, k == 2 * g + 1)
                return last

            pe.wait_ge(poolmat_ready, 1)
            pe.wait_ge(pool_lo_ready, TT)
            window(0)
            window(1)
            pe.wait_ge(pool_lo_ready, 2 * TT)
            window(2)
            pe.wait_ge(lo_ready, U_POOL + 1)
            pool_map(0)
            window(3)
            pool_map(1).then_inc(pooled, 1)
            pool_map(2)
            pool_map(3).then_inc(unit_used, 1)

            def logits(tiles):
                for k in tiles:
                    if k == 6:
                        pe.wait_ge(hT1_ready, 1)
                    elif k % 2 == 0:
                        pe.wait_ge(hT_ready, k // 2 + 1)
                    for t in range(TT):
                        last = nc.tensor.matmul(ps[2 * t][:, 0:E], hT[:, k, t * P:(t + 1) * P], router_g[:, k, :],
                                                start=k == 0, stop=k == KD - 1)
                return last

            pe.wait_ge(router_ready, 1)
            pe.wait_ge(pool_added, 2)
            turn(x, 0)
            turn(x, 1)
            logits(range(4))
            pe.wait_ge(pool_added, 4)
            turn(x, 2)
            turn(x, 3)
            logits(range(4, KD)).then_inc(logits_ready, 1)
            pe.wait_ge(sel_ready, 1)
            pe.wait_ge(consts_landed, CONSTS)
            for t in range(TT):
                for k in range(TT):
                    last = nc.tensor.matmul(ps[1][:, t * E:(t + 1) * E], before[:, k, t * P:(t + 1) * P], route[:, k, 4, :],
                                            start=k == 0, stop=k == TT - 1)
            last.then_inc(prefix_ready, 1)
            def gather(g):
                for n in range(2):
                    for src, bank in ((a_hi, ps[(3, 5)[n]]), (a_lo, ps[(2, 4)[n]])):
                        for q in range(4):
                            for t in range(TT):
                                c = t * D + (4 * n + q) * P
                                last = nc.tensor.matmul(bank[:, q * P:(q + 1) * P], src[:, c:c + P],
                                                        pick[:, t, :], start=t == 0, stop=t == TT - 1)
                        last.then_inc(gather_ready, 1)

            def turn_hidden(i, b):
                pe.wait_ge(h_ready, START + i * N_EB + b + 1)
                pe.wait_ge(hT_lo_ready, START + i * N_EB + b)
                if b == 0:
                    pe.wait_ge(x_added, START + 4 * i)
                for q in range(4):
                    last = nc.tensor.transpose(ps[6][:, q * P:(q + 1) * P], h[:, q * P:(q + 1) * P], ident[:, :])
                last.then_inc(htr_ready, 1)

            def expert(i, last_one):
                at = U_MOE + i * UE
                for j, (kind, b, half) in enumerate(MOE_SEQ):
                    u = U_MOE + j
                    if kind == "gate" and b == 0:
                        pe.wait_ge(xg_hi_ready, 2 * i + half + 1)
                        pe.wait_ge(xg_lo_ready, 2 * i + half + 1)
                    if kind == "gate" and half == 0:
                        if b == 1:
                            pe.wait_ge(x_added, START + 4 * i)
                        elif b:
                            pe.wait_ge(h_ready, START + i * N_EB + b - 1)
                    if kind == "down" and half == 0:
                        pe.wait_ge(hT_lo_ready, START + i * N_EB + b + 1)
                        if b == 0:
                            pe.wait_ge(y_lo_ready, START + 2 * i)
                    in_parts = last_one and j == UE - 1
                    if in_parts:
                        pe.wait_ge(first_lo_ready, (i + 1) // E)
                    else:
                        pe.wait_ge(lo_ready, at + j + 1)
                    if kind == "down":
                        h_hi, h_lo = hidden_T(b)
                        for k in range(2):
                            if in_parts and k:
                                pe.wait_ge(lo_ready, at + j + 1)
                            for n in range(2):
                                first = b == 0 and half == 0 and k == 0
                                final = b == N_EB - 1 and half == 1 and k == 1
                                last = product(ps[n][:, :], h_hi[:, 2 * half + k, :], h_lo[:, 2 * half + k, :],
                                               halves(u, k * D + n * 512, 512), first, final)
                                if in_parts and k and n == 0:
                                    last.then_inc(y_first_ready, 1)
                    else:
                        bank = ps[(2 if kind == "gate" else 4) + b % 2]
                        for k in range(4):
                            q = 4 * half + k
                            last = product(bank[:, :], xg_hi[:, q, :], xg_lo[:, q, :], halves(u, k * 512, 512),
                                           q == 0, q == KD - 1)
                    last.then_inc(unit_used, 1)
                    if kind == "gate" and half == 0 and b:
                        turn_hidden(i, b - 1)
                    if (kind, b, half) == ("up", 1, 0):
                        pe.wait_ge(x_added, START + 4 * i)
                        for t in range(TT):
                            last = nc.tensor.transpose(ps[7][:, t * P:(t + 1) * P], pick[:, t, :].bitcast(F32), ident[:, :])
                        last.then_inc(place_tr, 1)
                    if (kind, b, half) == ("down", N_EB - 2, 0):
                        turn_hidden(i, N_EB - 1)
                if not last_one:
                    pe.wait_ge(pick_ready, TT * (i + 2))
                    gather(i + 1)
                pe.wait_ge(place_ready, i + 1)
                for q, (n, t, bank) in enumerate(SCATTER):
                    if t == 0:
                        pe.wait_ge(y_lo_ready, START + 2 * i + n + 1)
                    if q == 2 and not last_one:
                        pe.wait_ge(xg_hi_ready, 2 * i + 4)
                    cols = slice(n * 512, (n + 1) * 512)
                    nc.tensor.matmul(ps[bank][:, :], place[:, t * P:(t + 1) * P], y_hi[:, cols], start=True, stop=False)
                    nc.tensor.matmul(ps[bank][:, :], place[:, t * P:(t + 1) * P], y_lo[:, cols], start=False, stop=True)\
                        .then_inc(scatter_ready, 1)

            def round_of_experts(first):
                pe.wait_ge(pick_ready, TT * (first + 1))
                if first:
                    pe.wait_ge(x_added, START + 4 * first)
                pe.wait_ge(hnsplit_hi, TT)
                pe.wait_ge(hnsplit_lo, TT)
                gather(first)
                if not first:
                    pe.wait_ge(over_ready, 1)
                    nc.tensor.matmul(ps[7][:, 0:1], ones[:, :], over[:, 0:1], start=True, stop=True)\
                        .then_inc(overs_summed, 1)
                with pe.Fori(0, E - 1) as e:
                    expert(e + first, False)
                expert(first + E - 1, True)

            pe.sem_inc(htr_ready, START)
            round_of_experts(0)
            pe.wait_ge(routed, 1)
            more = pe.value_load(over_i[0:1, 0:1], min_val=0, max_val=1)
            with pe.If(more != 0):
                round_of_experts(E)
                pe.nop()
            with pe.Else():
                pe.nop()


def shape_constants():
    import numpy as np

    order = np.arange(SEQ).reshape(16, 4, 4).transpose(2, 1, 0).reshape(-1)
    dist = order[:, None] - order[None, :]
    near = (dist >= 0) & (dist <= 128)
    by4 = (dist >= 0) & (dist % 4 == 0)
    by16 = (dist >= 0) & (dist % 16 == 0)
    mask = np.empty((TT, P, 4 * P), np.float32)
    for t in range(TT):
        rows = slice(t * P, (t + 1) * P)
        seen = np.concatenate([near[rows], by4[rows, rows], by16[rows, rows]], axis=1)
        mask[t] = np.where(seen, 0.0, MASKED)
    freq = (10000.0 ** (-np.arange(0, HD, 2, dtype=np.float32) / np.float32(HD))).astype(np.float32)
    angle = order[:, None].astype(np.float32) * freq[None, :]
    cos = np.concatenate([np.cos(angle)] * 4, axis=1).T.astype(np.float32)
    sin = np.concatenate([np.sin(angle), -np.sin(angle)] * 2, axis=1).T.astype(np.float32)
    pool = np.zeros((PG, SEQ, SEQ), np.float32)
    inv_count = np.zeros((SEQ, PG), np.float32)
    for g, size in enumerate(POOL_SIZES):
        count = np.minimum(order + 1, size).astype(np.float32)
        inside = (dist >= 0) & (dist < size)
        pool[g] = (inside - count[:, None] * np.eye(SEQ)).T
        inv_count[:, g] = 1 / count
    ident = np.eye(P, dtype=np.float32)
    iota = np.tile(np.arange(SEQ, dtype=np.float32), (P, 1))
    before = np.triu(np.ones((SEQ, SEQ), np.float32), 1)
    return order, dict(mask_in=mask, cos_in=cos, sin_in=sin, ident_in=ident, iota_in=iota,
                       before_in=before, poolmat_in=pool, inv_count_in=inv_count)


INPUTS = ("x", "mix_norm", "ffn_norm", "attn_w_qkv", "attn_w_o", "pool_w", "pool_scale", "dense_w_gate",
          "dense_w_up", "dense_w_down", "moe_router", "moe_w_gate", "moe_w_up", "moe_w_down", "final_norm")


def kernel(**inputs):
    import numpy as np
    import concourse.bacc as bacc
    from concourse import mybir as mb
    from concourse.bass_utils import run_bass_kernel_spmd

    order, constants = shape_constants()
    arrays = {name: np.ascontiguousarray(inputs[name]) for name in INPUTS}
    arrays["x"] = np.ascontiguousarray(arrays["x"][0][order])
    arrays.update(constants)
    columns = np.stack([arrays["mix_norm"][0], arrays["ffn_norm"][0], arrays["mix_norm"][1], arrays["ffn_norm"][1]])
    arrays["gain_col"] = np.ascontiguousarray(columns.reshape(4 * KD, P).T)
    del arrays["mix_norm"]
    nc = bacc.Bacc("TRN2", target_bir_lowering=False, num_devices=1)
    args = [nc.dram_tensor(f"in_{name}", a.shape, mb.dt.from_np(a.dtype), kind="ExternalInput").ap()
            for name, a in arrays.items()]
    args.append(nc.dram_tensor("out_0", (SEQ, D), F32, kind="ExternalOutput").ap())
    program(nc, *args)
    r = run_bass_kernel_spmd(nc, [{f"in_{name}": a for name, a in arrays.items()}], core_ids=[0])
    y = np.empty((1, SEQ, D), np.float32)
    y[0, order] = r.results[0]["out_0"]
    return y
```
